# Optimizing a Trainium2 kernel written in Bass

```python
import jax, jax.numpy as jnp
from jax import lax
import numpy as np

D_MODEL = 1024
BATCH = 1
SEQ = 512
DEPTH = 1

CHUNK = 64
EPS = 1e-6
D_RNN = 1024
RNN_BLOCKS = 8
RNN_BW = D_RNN // RNN_BLOCKS
CONV_W = 4
RG_C = 8.0
GLA_HEADS = 4
GLA_DK = 128
GLA_DV = 256
GLA_RANK = 16
GLA_TAU = 16.0
N_EXPERTS = 128
TOP_K = 8
D_EXPERT = 256
D_SHARED = 256
ROUTED_SCALE = 2.5
MOE_BLOCK = 64
IN_SPLITS = (D_RNN, D_RNN, GLA_HEADS * GLA_DK, GLA_HEADS * GLA_DK, GLA_HEADS * GLA_DV, GLA_HEADS * GLA_DV, GLA_RANK, D_MODEL, D_MODEL)
N_IN = 2 * D_RNN + 2 * GLA_HEADS * GLA_DK + 2 * GLA_HEADS * GLA_DV + GLA_RANK + 2 * D_MODEL

kernel_name = 'hybrid_rglru_gla_moe_adaln_encoder'

def _rmsnorm(x, g):
    xf = x.astype(jnp.float32)
    y = xf * lax.rsqrt(jnp.mean(xf * xf, axis=-1, keepdims=True) + EPS)
    return (y * g.astype(jnp.float32)).astype(x.dtype)

def _swiglu(x, w_gu, w_down):
    g, up = jnp.split(x @ w_gu, 2, axis=-1)
    return (jax.nn.silu(g) * up) @ w_down

def _causal_conv(x, w, b):
    s = x.shape[1]
    xp = jnp.pad(x, ((0, 0), (CONV_W - 1, 0), (0, 0)))
    y = b + xp[:, 0:s] * w[0]
    for j in range(1, CONV_W):
        y = y + xp[:, j:j + s] * w[j]
    return y

def _rglru(x, w_a, b_a, w_x, b_x, lam):
    bsz, s, _ = x.shape
    xb = x.reshape(bsz, s, RNN_BLOCKS, RNN_BW)
    r = jax.nn.sigmoid(jnp.einsum('bshi,hij->bshj', xb, w_a).reshape(bsz, s, D_RNN) + b_a)
    i = jax.nn.sigmoid(jnp.einsum('bshi,hij->bshj', xb, w_x).reshape(bsz, s, D_RNN) + b_x)
    log_a = -RG_C * r.astype(jnp.float32) * jax.nn.softplus(-lam.astype(jnp.float32))
    a = jnp.exp(log_a)
    mult = jnp.sqrt(-jnp.expm1(2.0 * log_a))
    mult = jnp.where((jnp.arange(s) == 0)[None, :, None], 1.0, mult)
    bt = mult * (i * x).astype(jnp.float32)

    def combine(p, q):
        return p[0] * q[0], q[0] * p[1] + q[1]

    _, h = lax.associative_scan(combine, (a, bt), axis=1)
    return h.astype(x.dtype)

def _gla(q, k, v, log_alpha):
    bsz, s = q.shape[:2]
    nc = s // CHUNK
    f32 = jnp.float32

    def chunks(t):
        return t.astype(f32).reshape(bsz, nc, CHUNK, *t.shape[2:]).swapaxes(0, 1)

    cum = jnp.cumsum(chunks(log_alpha), axis=2)
    tot = cum[:, :, -1]
    k_dec = chunks(k) * jnp.exp(tot[:, :, None] - cum)

    def step(state, inp):
        qc, kc, vc, tc = inp
        state = jnp.exp(tc)[..., None] * state + jnp.einsum('bchk,bchv->bhkv', kc, vc)
        return state, jnp.einsum('bchk,bhkv->bchv', qc, state)

    s0 = jnp.zeros((bsz, GLA_HEADS, GLA_DK, GLA_DV), f32)
    _, o = lax.scan(step, s0, (chunks(q), k_dec, chunks(v), tot))
    return o.swapaxes(0, 1).reshape(bsz, s, GLA_HEADS, GLA_DV).astype(q.dtype)

def _mixer(u, w_in, conv_w, conv_b, rg_wa, rg_ba, rg_wx, rg_bx, rg_lambda,
           gla_w_up, gla_b_up, gla_norm_g, w_branch_a, w_branch_b, w_out):
    bsz, s, _ = u.shape
    w_rx, w_rg, w_q, w_k, w_v, w_og, w_lr, w_ga, w_gb = jnp.split(
        w_in, np.cumsum(IN_SPLITS)[:-1].tolist(), axis=1)
    xr = _causal_conv(u @ w_rx, conv_w, conv_b)
    h_rnn = _rglru(xr, rg_wa, rg_ba, rg_wx, rg_bx, rg_lambda)
    y_a = (h_rnn * jax.nn.gelu(u @ w_rg, approximate=True)) @ w_branch_a
    q = (u @ w_q).reshape(bsz, s, GLA_HEADS, GLA_DK) * (GLA_DK ** -0.5)
    k = (u @ w_k).reshape(bsz, s, GLA_HEADS, GLA_DK)
    v = (u @ w_v).reshape(bsz, s, GLA_HEADS, GLA_DV)
    gate_logit = ((u @ w_lr) @ gla_w_up + gla_b_up).astype(jnp.float32)
    log_alpha = (jax.nn.log_sigmoid(gate_logit) / GLA_TAU).reshape(bsz, s, GLA_HEADS, GLA_DK)
    o = _gla(q, k, v, log_alpha)
    o = _rmsnorm(o, gla_norm_g).reshape(bsz, s, GLA_HEADS * GLA_DV) * jax.nn.silu(u @ w_og)
    y_b = o @ w_branch_b
    m = jax.nn.sigmoid(u @ w_ga) * y_a + jax.nn.sigmoid(u @ w_gb) * y_b
    return m @ w_out

def _routed_experts(u, idx, wts, w_gu, w_down):
    s, d = u.shape
    m = s * TOP_K
    nb = -(-(m + N_EXPERTS * (MOE_BLOCK - 1)) // MOE_BLOCK)
    p = nb * MOE_BLOCK
    e_flat = idx.reshape(m)
    order = jnp.argsort(e_flat, stable=True)
    e_sorted = e_flat[order]
    tok_sorted = (order // TOP_K).astype(jnp.int32)
    w_sorted = wts.reshape(m)[order]
    counts = jnp.bincount(e_flat, length=N_EXPERTS)
    padded = (counts + MOE_BLOCK - 1) // MOE_BLOCK * MOE_BLOCK
    start = jnp.cumsum(counts) - counts
    ends_p = jnp.cumsum(padded)
    pstart = ends_p - padded
    dest = pstart[e_sorted] + jnp.arange(m) - start[e_sorted]
    row_tok = jnp.full((p,), s, jnp.int32).at[dest].set(tok_sorted)
    row_w = jnp.zeros((p,), wts.dtype).at[dest].set(w_sorted)
    block_exp = jnp.minimum(jnp.searchsorted(ends_p, jnp.arange(nb) * MOE_BLOCK, side='right'), N_EXPERTS - 1)
    u_pad = jnp.concatenate([u, jnp.zeros((1, d), u.dtype)], axis=0)[row_tok].reshape(nb, MOE_BLOCK, d)

    def group_fn(args):
        xg, e = args
        return _swiglu(xg, w_gu[e], w_down[e])

    y = lax.map(group_fn, (u_pad, block_exp)).reshape(p, d)
    return jnp.zeros((s + 1, d), u.dtype).at[row_tok].add(y * row_w[:, None])[:s]

def _moe(u, router_w, router_b, exp_w_gu, exp_w_down, shared_w_gu, shared_w_down):
    scores = jax.nn.sigmoid((u @ router_w).astype(jnp.float32))
    _, idx = lax.top_k(scores + router_b.astype(jnp.float32), TOP_K)
    s_sel = jnp.take_along_axis(scores, idx, axis=-1)
    wts = (s_sel / jnp.sum(s_sel, axis=-1, keepdims=True) * ROUTED_SCALE).astype(u.dtype)
    routed = lax.map(lambda a: _routed_experts(a[0], a[1], a[2], exp_w_gu, exp_w_down), (u, idx, wts))
    return routed + _swiglu(u, shared_w_gu, shared_w_down)

def setup_inputs(seed: int = 0) -> dict:
    key = jax.random.key(seed)
    ks = jax.random.split(key, 32)
    L, D = DEPTH, D_MODEL

    def nrm(k, shape, scale):
        return jax.random.normal(k, shape, jnp.float32) * scale

    def gain(k, shape):
        return 1.0 + 0.02 * jax.random.normal(k, shape, jnp.float32)

    a_pow = jax.random.uniform(ks[12], (L, D_RNN), jnp.float32, minval=0.9, maxval=0.999)
    a0 = a_pow ** (1.0 / RG_C)
    rg_lambda = jnp.log(a0) - jnp.log1p(-a0)
    return {
        'x': nrm(ks[0], (BATCH, SEQ, D), 1.0),
        'c': nrm(ks[1], (BATCH, D), 1.0),
        'ada_w': nrm(ks[2], (L, D, 6 * D), 0.5 * D ** -0.5),
        'ada_b': nrm(ks[3], (L, 6 * D), 0.02),
        'norm1_g': gain(ks[4], (L, D)),
        'w_in': nrm(ks[5], (L, D, N_IN), D ** -0.5),
        'conv_w': nrm(ks[6], (L, CONV_W, D_RNN), CONV_W ** -0.5),
        'conv_b': nrm(ks[7], (L, D_RNN), 0.02),
        'rg_wa': nrm(ks[8], (L, RNN_BLOCKS, RNN_BW, RNN_BW), RNN_BW ** -0.5),
        'rg_ba': nrm(ks[9], (L, D_RNN), 0.02),
        'rg_wx': nrm(ks[10], (L, RNN_BLOCKS, RNN_BW, RNN_BW), RNN_BW ** -0.5),
        'rg_bx': nrm(ks[11], (L, D_RNN), 0.02),
        'rg_lambda': rg_lambda,
        'gla_w_up': nrm(ks[13], (L, GLA_RANK, GLA_HEADS * GLA_DK), GLA_RANK ** -0.5),
        'gla_b_up': nrm(ks[14], (L, GLA_HEADS * GLA_DK), 0.02),
        'gla_norm_g': gain(ks[15], (L, GLA_HEADS, GLA_DV)),
        'w_branch_a': nrm(ks[16], (L, D_RNN, D), D_RNN ** -0.5),
        'w_branch_b': nrm(ks[17], (L, GLA_HEADS * GLA_DV, D), (GLA_HEADS * GLA_DV) ** -0.5),
        'w_out': nrm(ks[18], (L, D, D), D ** -0.5),
        'norm2_g': gain(ks[19], (L, D)),
        'router_w': nrm(ks[20], (L, D, N_EXPERTS), D ** -0.5),
        'router_b': nrm(ks[21], (L, N_EXPERTS), 0.01),
        'exp_w_gu': nrm(ks[22], (L, N_EXPERTS, D, 2 * D_EXPERT), D ** -0.5),
        'exp_w_down': nrm(ks[23], (L, N_EXPERTS, D_EXPERT, D), D_EXPERT ** -0.5),
        'shared_w_gu': nrm(ks[24], (L, D, 2 * D_SHARED), D ** -0.5),
        'shared_w_down': nrm(ks[25], (L, D_SHARED, D), D_SHARED ** -0.5),
        'final_g': gain(ks[26], (D,)),
    }

def reference(x, c, ada_w, ada_b, norm1_g, w_in, conv_w, conv_b, rg_wa, rg_ba, rg_wx, rg_bx,
              rg_lambda, gla_w_up, gla_b_up, gla_norm_g, w_branch_a, w_branch_b, w_out, norm2_g,
              router_w, router_b, exp_w_gu, exp_w_down, shared_w_gu, shared_w_down, final_g):
    h = x
    c_act = jax.nn.silu(c)
    for l in range(DEPTH):
        mod = (c_act @ ada_w[l] + ada_b[l])[:, None, :]
        sh1, sc1, g1, sh2, sc2, g2 = jnp.split(mod, 6, axis=-1)
        u = _rmsnorm(h, norm1_g[l]) * (1 + sc1) + sh1
        h = h + g1 * _mixer(u, w_in[l], conv_w[l], conv_b[l], rg_wa[l], rg_ba[l], rg_wx[l], rg_bx[l],
                            rg_lambda[l], gla_w_up[l], gla_b_up[l], gla_norm_g[l],
                            w_branch_a[l], w_branch_b[l], w_out[l])
        u = _rmsnorm(h, norm2_g[l]) * (1 + sc2) + sh2
        h = h + g2 * _moe(u, router_w[l], router_b[l], exp_w_gu[l], exp_w_down[l],
                          shared_w_gu[l], shared_w_down[l])
    return _rmsnorm(h, final_g)


_drawn_inputs = setup_inputs


def setup_inputs(seed=0):
    import zlib

    import numpy as np

    out = dict(_drawn_inputs(seed))
    spreads = {}
    factors = {'norm1_g': 3.348,
     'rg_ba': 49.061,
     'rg_bx': 37.958,
     'gla_b_up': 7.915,
     'gla_norm_g': 22.325,
     'final_g': 7.63,
     'conv_b': 4.903,
     'norm2_g': 6.638,
     'router_b': 4.176}
    for name, (base, spread) in spreads.items():
        noise = np.random.default_rng([zlib.crc32(name.encode()), seed]).standard_normal(out[name].shape)
        drawn = base * np.exp(spread * noise) if base else spread * noise
        out[name] = __import__('jax').numpy.asarray(drawn.astype(out[name].dtype))
    for name, factor in factors.items():
        out[name] = (out[name] * factor).astype(out[name].dtype)
    return out
```

```python
from contextlib import ExitStack

import concourse.bass as bass
from concourse import mybir

ALU = mybir.AluOpType
ACT = mybir.ActivationFunctionType
F32 = mybir.dt.float32
BF16 = mybir.dt.bfloat16
U32 = mybir.dt.uint32
AX_X = mybir.AxisListType.X

P = 128
T = 512
TT = T // P
D = 1024
KT = D // P
NC = 512
CHUNK = 64
NCHUNK = T // CHUNK
HEADS = 4
DK = 128
DV = 256
RANK = 16
RNN_BLOCKS = 8
CONV_W = 4
RG_C = 8.0
EPS = 1e-6
E = 128
TOP_K = 8
DE = 256
MOE_BLOCKS = (T * TOP_K - E) // P + E
UNROLL, SPAN = 3, 6
SPANS = -(-MOE_BLOCKS // (UNROLL * SPAN))
TABLE = SPANS * SPAN * UNROLL + UNROLL
ROUTED_SCALE = 2.5
BANKS = 8

W_RX, W_RG, W_Q, W_K, W_V, W_OG, W_LR, W_GA, W_GB = 0, 1024, 2048, 2560, 3072, 4096, 5120, 5136, 6160


def plan():
    jobs = [("vectors", "dve")]
    jobs += [(("ada", c), "dve") for c in range(4)]
    jobs += [(("uT", t, g), "act") for t in range(TT) for g in range(2)]
    jobs += [("lr", "act")]
    jobs += [(("gate", t), "dve") for t in range(TT)]
    jobs += [(("v", n, t), "act") for n in range(2) for t in range(TT)]
    jobs += [(("rem", t), "act") for t in range(TT)]
    jobs += [("tot", "act")]
    jobs += [(("k", t), "dve") for t in range(TT)]
    jobs += [(("q", h), "act") for h in range(HEADS)]
    for c in range(NCHUNK + 1):
        if c < NCHUNK:
            jobs += [(("kv", c, g), "dve") for g in range(2)]
        if c >= 1:
            jobs += [(("o", c - 1), "act")]
    jobs += [(("rg", j), "act") for j in range(KT)]
    jobs += [(("ss", h), "act") for h in range(HEADS)]
    jobs += [(("og", j), "act") for j in range(KT)]
    for n in range(2):
        jobs += [(("rx", j), "dve") for j in range(4 * n, 4 * n + 4)]
        jobs += [((g, j), "act") for j in range(4 * n, 4 * n + 4) for g in ("ra", "ri")]
        jobs += [(("ada", c), "dve") for c in range(4 + 4 * n, 8 + 4 * n)]
    for gate, y in (("gb", "yb"), ("ga", "ya")):
        for n in range(2):
            jobs += [((gate, j), "act") for j in range(4 * n, 4 * n + 4)]
            jobs += [((y, j), "dve") for j in range(4 * n, 4 * n + 4)]
    jobs += [(("out", n, t), "dve") for n in range(2) for t in range(TT)]
    jobs += [(("u2T", t, g), "act") for t in range(TT) for g in range(2)]
    jobs += [(("router", t), "act") for t in range(TT)]
    jobs += [(("sgu", t), "dve") for t in range(TT)]
    jobs += [("count", "dve"), ("pos", "dve"), ("bstart_col", "dve"), ("bstart_row", "dve"), ("table", "dve")]
    jobs += [(("shT", t), "act") for t in range(TT)]
    jobs += [(("sdown", n, t), "act") for n in range(2) for t in range(TT)]
    return jobs


def layer_program(nc, x, c, ada_w, ada_b, norm1_g, w_in, conv_w, conv_b, rg_wa, rg_ba, rg_wx, rg_bx,
                  rg_lambda, gla_w_up, gla_b_up, gla_norm_g, w_branch_a, w_branch_b, w_out, norm2_g,
                  router_w, router_b, exp_w_gu, exp_w_down, shared_w_gu, shared_w_down, final_g, out):
    jobs = plan()
    J = {name: n for n, (name, _) in enumerate(jobs)}
    emptied_by = [engine for _, engine in jobs]
    emptied_n = [emptied_by[:n + 1].count(emptied_by[n]) for n in range(len(jobs))]

    with ExitStack() as ctx:
        def sb(name, shape, dt=F32, where=ctx):
            return where.enter_context(nc.sbuf_tensor(name, shape, dt))

        def sem(name):
            return ctx.enter_context(nc.semaphore(name))

        psum = ctx.enter_context(nc.psum_tensor("psum", [P, BANKS, NC], F32))

        u2_dram = nc.dram_tensor("u2_rows", (T, D), F32, kind="Internal").ap()
        sum_dram = nc.dram_tensor("expert_sum", (T + P, D), F32, kind="Internal").ap()

        x_tok = sb("x_tok", [P, TT, D])
        ident = sb("ident", [P, P])
        ones = sb("ones", [P, P])
        tri = sb("tri", [P, P], BF16)
        ones_b = sb("ones_b", [P, P], BF16)
        iota_row = sb("iota_row", [P, P])
        block_start = sb("block_start", [P, TABLE])
        eps = sb("eps", [P, 1])
        step_word = sb("step_word", [1, 1])
        dummy_row = sb("dummy_row", [P, 1])
        stat = sb("stat", [P, 8])
        rstd = sb("rstd", [P, 8])
        mods = sb("mods", [P, 8, NC])
        g2_row = mods[:, 6:8, :].rearrange("p a b -> p (a b)")
        ring = sb("ring", [P, 2, KT, NC])
        row_a = sb("row_a", [P, D])
        tmp_tok = sb("tmp_tok", [P, 2, D])

        mix = ExitStack()
        uT = sb("uT", [P, KT, T], F32, mix)
        oT = sb("oT", [P, KT, T], F32, mix)
        hgT = sb("hgT", [P, KT, T], F32, mix)
        v_tok = sb("v_tok", [P, TT, D], F32, mix)
        mT = v_tok[:, :, :].rearrange("p t (a n) -> p (t a) n", a=2)
        er = sb("er", [P, TT, NC], F32, mix)
        qT = sb("qT", [P, HEADS, T], F32, mix)
        la = sb("la", [P, TT, NC], F32, mix)
        xr = sb("xr", [P, 4, T], F32, mix)
        tau = sb("tau", [P, 4, T], F32, mix)
        tmpT = sb("tmpT", [P, 4, T], F32, mix)
        sh1sc1 = la
        wlr = sb("wlr", [P, KT, RANK], F32, mix)
        lrT = hgT[0:32, 0, :]
        wup = hgT[0:32, 1, :]
        gate_w = sb("gate_w", [P, 2, RNN_BLOCKS, P], F32, mix)
        t1, t2 = tmp_tok[:, 1, 0:T], tmp_tok[:, 1, T:2 * T]
        vec_rows = oT[0:72, 0, 0:P]
        vec = sb("vec", [P, 72], F32, mix)
        sp4 = sb("sp4", [P, 16], F32, mix)
        c_col = sb("c_col", [P, KT], F32, mix)
        c_rep = sb("c_rep", [P, KT, P], F32, mix)
        decay = sb("decay", [P, HEADS, NCHUNK], F32, mix)
        later = sb("later", [P, P], F32, mix)
        in_chunk = sb("in_chunk", [P, 2], F32, mix)
        state = tmp_tok[:, :, :].rearrange("p s (h v) -> p s h v", h=HEADS)
        CW, CB, BA, BX, LAM, GN = 0, 32, 40, 48, 56, 64
        mix.close()

        moe = ExitStack()
        w_gu = sb("w_gu", [P, UNROLL, KT, 2 * DE], F32, moe)
        w_dn = sb("w_dn", [P, UNROLL, 2, D], F32, moe)
        u2T = sb("u2T", [P, KT, T], F32, moe)
        xg = sb("xg", [P, UNROLL, D], F32, moe)
        xT = sb("xT", [P, KT, P], F32, moe)
        y_rows = sb("y_rows", [P, D], F32, moe)
        router = sb("router", [P, KT, E], F32, moe)
        bias_row = sb("bias_row", [P, E], F32, moe)
        scores = sb("scores", [P, TT, E], F32, moe)
        sel = sb("sel", [P, TT, E], F32, moe)
        slot = sb("slot", [P, TT, E], F32, moe)
        mask = sb("mask", [P, TT, E], F32, moe)
        mask_b = sb("mask_b", [P, TT, E], BF16, moe)
        top8 = sb("top8", [P, TT, TOP_K], F32, moe)
        w3 = sb("w3", [P, TT, E, 3], BF16, moe)
        w_left = sb("w_left", [P, TT, E], F32, moe)
        n_col = sb("n_col", [P, 8], F32, moe)
        nb_rep = sb("nb_rep", [P, P], BF16, moe)
        over = sb("over", [P, TABLE], BF16, moe)
        expert_of = sb("expert_of", [1, TABLE], U32, moe)
        live_of = sb("live_of", [1, TABLE], U32, moe)
        pick = scores[:, 0:2].bitcast(BF16).rearrange("p a (b n) -> p (a b) n", b=2)
        pick_cols = sb("pick_cols", [P, TT, 5], BF16, moe)
        tok_cols = sb("tok_cols", [P, TT, 2], F32, moe)
        got = sb("got", [P, 8], F32, moe)
        row_idx = sb("row_idx", [P, UNROLL, 1], U32, moe)
        add_idx = sb("add_idx", [P, UNROLL, 1], U32, moe)
        live_count = sb("live_count", [1, 1], U32, moe)
        row_w = sb("row_w", [P, UNROLL], F32, moe)
        gate_h = sel[:, 0:2].rearrange("p a n -> p (a n)")
        h_tok = sel[:, 2:4].rearrange("p a n -> p (a n)")
        hT = mask[:, 0:2]
        live_row = xT[0:1, 0:2].rearrange("p a n -> p (a n)")[:, 0:TABLE]
        sgate = xT[:, 0:2].rearrange("p a n -> p (a n)")
        sum_tok = u2T[:, :, :].rearrange("p (t a) n -> p t (a n)", a=2)
        moe.close()

        job_done = sem("job_done")
        act_emptied = sem("act_emptied")
        dve_emptied = sem("dve_emptied")
        act_own = sem("act_own")
        dve_own = sem("dve_own")
        pool_own = sem("pool_own")
        consts_ready = sem("consts_ready")
        x_in = sem("x_in")
        small_in = sem("small_in")
        rows_in = sem("rows_in")
        chunk_in = [sem(f"chunk_in{s}") for s in range(2)]
        gates_in = sem("gates_in")
        c_ready = sem("c_ready")
        c_rep_ready = sem("c_rep_ready")
        sums1, sums2, sums3 = [sem(f"sums{i}") for i in (1, 2, 3)]
        roots1, roots2, roots3 = [sem(f"roots{i}") for i in (1, 2, 3)]
        u_ready = sem("u_ready")
        gate_ready = sem("gate_ready")
        log_ready = sem("log_ready")
        la_ready = sem("la_ready")
        state_ready = sem("state_ready")
        sq_ready = sem("sq_ready")
        root_ready = sem("root_ready")
        silu_og = sem("silu_og")
        og_used = sem("og_used")
        conv_ready = sem("conv_ready")
        sp_ready = sem("sp_ready")
        ri_ready = sem("ri_ready")
        tau_ready = sem("tau_ready")
        sqrt_ready = sem("sqrt_ready")
        rg_done = sem("rg_done")
        o_ready = sem("o_ready")
        m_ready = sem("m_ready")
        h_res = sem("h_res")
        n2_in = sem("n2_in")
        u2_ready = sem("u2_ready")
        u2_out = [sem(f"u2_out{s}") for s in range(2)]
        fg_in = sem("fg_in")
        router_in = sem("router_in")
        score_ready = sem("score_ready")
        mask_ready = sem("mask_ready")
        nb_ready = sem("nb_ready")
        over_ready = sem("over_ready")
        tables_ready = sem("tables_ready")
        sgate_ready = sem("sgate_ready")
        sh_ready = sem("sh_ready")
        xg_zero = sem("xg_zero")
        w_loaded = [sem(f"w_loaded{s}") for s in range(UNROLL)]
        pick_ready = sem("pick_ready")
        idx_psum = sem("idx_psum")
        idx_ready = sem("idx_ready")
        gathered = [sem(f"gathered{s}") for s in range(UNROLL)]
        xT_psum = sem("xT_psum")
        xT_ready = sem("xT_ready")
        gu_done = sem("gu_done")
        silu_done = sem("silu_done")
        h_ready = sem("h_ready")
        hT_psum = sem("hT_psum")
        hT_ready = sem("hT_ready")
        y_psum = sem("y_psum")
        y_ready = sem("y_ready")
        scattered = sem("scattered")
        experts_done = sem("experts_done")
        found = sem("found")
        add_ready = sem("add_ready")
        step_done = sem("step_done")
        sum_started = sem("sum_started")
        h2_res = sem("h2_res")
        sum_in = sem("sum_in")
        out_ready = sem("out_ready")
        stored = sem("stored")

        def bank(name):
            return psum[:, J[name] % BANKS, :]

        def wait_job(eng, name):
            eng.wait_ge(job_done, J[name] + 1)

        def wait_emptied(eng, name):
            n = J[name]
            eng.wait_ge(act_emptied if emptied_by[n] == "act" else dve_emptied, emptied_n[n])

        class Own:
            def __init__(self, eng, s):
                self.eng, self.s, self.n = eng, s, 0

            def __call__(self, ins):
                self.n += 1
                ins.then_inc(self.s, 1)

            def settle(self):
                self.eng.wait_ge(self.s, self.n)

        wl = w_in[0]
        k_major = lambda w: w.rearrange("(k p) n -> p k n", p=P)
        chunks = [(("ada", i), k_major(ada_w[0])[:, :, i * NC:(i + 1) * NC], ("ada", i)) for i in range(4)]
        chunks += [(("v", n), k_major(wl)[:, :, W_V + n * NC:W_V + (n + 1) * NC], ("v", n, TT - 1)) for n in range(2)]
        chunks += [("k", k_major(wl)[:, :, W_K:W_K + NC], ("k", TT - 1)),
                   ("q", k_major(wl)[:, :, W_Q:W_Q + NC], ("q", HEADS - 1))]
        for name, col in (("rg", W_RG), ("og", W_OG)):
            chunks += [((name, n), k_major(wl)[:, :, col + n * NC:col + (n + 1) * NC], (name, 4 * n + 3)) for n in range(2)]
        for n in range(2):
            chunks += [(("rx", n), k_major(wl)[:, :, W_RX + n * NC:W_RX + (n + 1) * NC], ("rx", 4 * n + 3))]
            chunks += [(("ada", i), k_major(ada_w[0])[:, :, i * NC:(i + 1) * NC], ("ada", i)) for i in range(4 + 4 * n, 8 + 4 * n)]
        for gate, y, col, w in (("gb", "yb", W_GB, w_branch_b), ("ga", "ya", W_GA, w_branch_a)):
            for n in range(2):
                chunks += [((gate, n), k_major(wl)[:, :, col + n * NC:col + (n + 1) * NC], (gate, 4 * n + 3)),
                           ((y, n), k_major(w[0])[:, :, n * NC:(n + 1) * NC], (y, 4 * n + 3))]
        chunks += [(("out", n), k_major(w_out[0])[:, :, n * NC:(n + 1) * NC], ("out", n, TT - 1)) for n in range(2)]
        chunks += [("sgu", k_major(shared_w_gu[0]), ("sgu", TT - 1))]
        chunks += [("sdown", shared_w_down[0].rearrange("(j p) n -> p j n", p=P), ("sdown", 1, TT - 1))]
        C = {name: n for n, (name, _, _) in enumerate(chunks)}

        def chunk(name):
            return ring[:, C[name] % 2]

        def wait_chunk(eng, name):
            eng.wait_ge(chunk_in[C[name] % 2], 16 * (C[name] // 2 + 1))

        sdown_w = ring[:, C["sdown"] % 2, 0:4].rearrange("p (j a) n -> p j (a n)", j=2)
        sh_tok = ring[:, C["sdown"] % 2, 4:6].rearrange("p a (t n) -> p (a t) n", n=DE)
        shT = ring[:, C["sdown"] % 2, 6:8]

        expert_gu = exp_w_gu[0].rearrange("e (p k) f -> e p k f", k=KT)
        expert_dn = exp_w_down[0].rearrange("e (j p) n -> e p j n", p=P)
        x_rows = x[0].rearrange("(t p) d -> p t d", p=P)
        SMALL = 7
        GU, HT, IDX, Y0 = 2, 3, 4, 5
        moe_bank = lambda n: psum[:, n, :]

        def live_blocks(eng, ask=True):
            with eng.Fori(0, SPANS) as span:
                live_span = eng.value_load(live_of[0:1, bass.ds(span * (SPAN * UNROLL), 1)], min_val=0, max_val=1)
                with eng.If(live_span > 0):
                    with eng.Fori(0, SPAN) as group:
                        i = span * SPAN + group
                        for s in range(UNROLL):
                            b = i * UNROLL + s
                            if not ask:
                                yield i, s, b
                                continue
                            live = eng.value_load(live_of[0:1, bass.ds(b, 1)], min_val=0, max_val=1)
                            with eng.If(live > 0):
                                yield i, s, b
                    eng.nop()

        block = ctx.enter_context(nc.Block())

        @block.sync
        def _(sp):
            for n, (name, src, _) in enumerate(chunks):
                if n >= 2:
                    wait_job(sp, chunks[n - 2][2])
                dst = sdown_w if name == "sdown" else ring[:, n % 2]
                sp.dma_start(dst, src).then_inc(chunk_in[n % 2], 16)
            wait_job(sp, ("out", 1, TT - 1))
            wait_emptied(sp, ("out", 1, TT - 1))
            sp.wait_ge(tables_ready, 1)

            def load_expert(b, s, done=None):
                live = sp.value_load(live_of[0:1, bass.ds(b, 1)], min_val=0, max_val=1)
                with sp.If(live > 0):
                    e = sp.value_load(expert_of[0:1, bass.ds(b, 1)], min_val=0, max_val=E - 1)
                    if done is not None:
                        sp.wait_ge(y_psum, done)
                    sp.dma_start(w_gu[:, s], expert_gu[bass.ds(e, 1)].rearrange("o p k f -> p (o k) f")).then_inc(w_loaded[s], 16)
                    sp.dma_start(w_dn[:, s], expert_dn[bass.ds(e, 1)].rearrange("o p j n -> p (o j) n")).then_inc(w_loaded[s], 16)

            for b in range(UNROLL):
                load_expert(b, b)
            for i, s, b in live_blocks(sp, ask=False):
                load_expert(b + UNROLL, s, 2 * b + 4)
            sp.wait_ge(experts_done, 1)
            sp.dma_start(sum_tok, sum_dram[0:T].rearrange("(t p) d -> p t d", p=P)).then_inc(sum_in, 16)
            for t in range(TT):
                sp.wait_ge(out_ready, t + 1)
                sp.dma_start(out[0].rearrange("(t p) d -> p t d", p=P)[:, t], x_tok[:, t]).then_inc(stored, 16)
            sp.wait_ge(stored, 16 * TT)

        @block.gpsimd
        def _(pool):
            count = Own(pool, pool_own)

            def own(ins):
                count(ins)
                count.settle()

            own(pool.memset(ident[:], 0.0))
            own(pool.memset(ones[:], 1.0))
            own(pool.memset(ones_b[:], 1.0))
            own(pool.memset(later[:], 1.0))
            own(pool.memset(tri[:], 1.0))
            own(pool.memset(in_chunk[:], 0.0))
            own(pool.memset(eps[:], EPS))
            own(pool.memset(lrT, 1.0))
            own(pool.affine_select(ident[:], ident[:], [[-1, P]], ALU.not_equal, 1.0, base=0, channel_multiplier=1))
            own(pool.affine_select(later[:], later[:], [[-1, P]], ALU.is_gt, 0.0, base=0, channel_multiplier=1))
            own(pool.affine_select(tri[:], tri[:], [[1, P]], ALU.is_gt, 0.0, base=0, channel_multiplier=-1))
            own(pool.memset(in_chunk[0:CHUNK, 0:1], 1.0))
            own(pool.memset(in_chunk[CHUNK:P, 1:2], 1.0))
            own(pool.iota(iota_row[:], [[1, P]], base=0, channel_multiplier=0, allow_small_or_imprecise_dtypes=True))
            own(pool.iota(block_start[:], [[P, TABLE]], base=0, channel_multiplier=0, allow_small_or_imprecise_dtypes=True))
            own(pool.iota(dummy_row[:], [[0, 1]], base=T + 1, channel_multiplier=1, allow_small_or_imprecise_dtypes=True))
            own(pool.memset(later[CHUNK:P, 0:CHUNK], 0.0))
            pool.nop().then_inc(consts_ready, 1)
            pool.wait_ge(c_ready, 1)
            for k in range(KT):
                own(pool.tensor_scalar(c_rep[:, k], ones[:], c_col[:, k:k + 1], None, ALU.mult))
            pool.nop().then_inc(c_rep_ready, 1)

            wait_job(pool, ("out", 1, TT - 1))
            pool.memset(xg[:], 0.0).then_inc(xg_zero, 1)
            own(pool.iota(tok_cols[:, :, 0:1], [[0, TT], [0, 1]], base=1, channel_multiplier=1, allow_small_or_imprecise_dtypes=True))
            own(pool.iota(tok_cols[:, :, 1:2], [[P, TT], [0, 1]], base=0, channel_multiplier=0, allow_small_or_imprecise_dtypes=True))
            pool.nop().then_inc(xg_zero, 1)
            for t in range(2):
                pool.wait_ge(u2_out[t % 2], 32)
            pool.wait_ge(sum_started, 16)
            pool.wait_ge(xg_zero, 1)
            pool.dma_start(sum_dram[T:T + P], xg[:, 0]).then_inc(scattered, 16)
            pool.wait_ge(scattered, 16)
            pool.wait_ge(tables_ready, 1)

            def step(n):
                if not isinstance(n, int) or n > 0:
                    pool.wait_ge(step_done, n)
                pool.tensor_tensor(step_word[:], ones[0:1, 0:1], ones[0:1, 0:1], ALU.mult).then_inc(step_done, 1)

            def gather(b, s, n):
                pool.wait_ge(idx_ready, b + 1)
                step(n)
                pool.indirect_dma_start(xg[:, s], None, u2_dram, bass.IndirectOffsetOnAxis(row_idx[:, s], 0),
                                        bounds_check=T - 1, oob_is_err=False).then_inc(gathered[s], 16)

            gather(0, 0, 0)
            gather(1, 1, 1)
            for i, s, b in live_blocks(pool):
                pool.wait_ge(xT_psum, 2 * b + 2)
                gather(b + 2, (s + 2) % UNROLL, 2 * b + 2)
                pool.wait_ge(scattered, 16 * b + 16)
                pool.wait_ge(y_ready, 2 * b + 4)
                pool.wait_ge(add_ready, b + 1)
                step(2 * b + 3)
                pool.indirect_dma_start(sum_dram, bass.IndirectOffsetOnAxis(add_idx[:, s], 0), y_rows[:], None,
                                        compute_op=ALU.add, bounds_check=T + P - 1, oob_is_err=True).then_inc(scattered, 16)
            live_n = pool.value_load(live_count[0:1, 0:1], min_val=1, max_val=MOE_BLOCKS)
            pool.wait_ge(scattered, 16 * live_n + 16)
            pool.wait_ge(step_done, 2 * live_n + 2)
            pool.tensor_tensor(step_word[:], ones[0:1, 0:1], ones[0:1, 0:1], ALU.mult).then_inc(experts_done, 1)

        @block.scalar
        def _(act):
            own = Own(act, act_own)
            act.dma_start(x_tok[:], x_rows).then_inc(x_in, 16)
            act.dma_start(c_col[:], c.rearrange("o (k p) -> p (o k)", p=P), allow_slow_non_contiguous=True).then_inc(small_in, 16)
            act.dma_start(vec_rows[CW:CW + 32, :], conv_w[0].rearrange("j (k p) -> (j k) p", p=P)).then_inc(rows_in, 16)
            for at, v in ((CB, conv_b), (BA, rg_ba), (BX, rg_bx), (LAM, rg_lambda)):
                act.dma_start(vec_rows[at:at + 8, :], v.rearrange("o (k p) -> (o k) p", p=P)).then_inc(rows_in, 16)
            act.dma_start(vec_rows[GN:GN + 8, :], gla_norm_g[0].rearrange("h (k p) -> (h k) p", p=P)).then_inc(rows_in, 16)
            act.dma_start(row_a[:], norm1_g.broadcast_to([P, D])).then_inc(small_in, 16)
            act.dma_start(sh1sc1[:].rearrange("p a n -> p (a n)"), ada_b[:, 0:4 * NC].broadcast_to([P, 4 * NC])).then_inc(small_in, 16)
            act.dma_start(mods[:].rearrange("p a n -> p (a n)"), ada_b[:, 4 * NC:12 * NC].broadcast_to([P, 8 * NC])).then_inc(small_in, 16)
            act.dma_start(wlr[:], k_major(wl)[:, :, W_LR:W_LR + RANK]).then_inc(small_in, 16)
            act.dma_start(wup[0:RANK, :], gla_w_up[0]).then_inc(small_in, 16)
            act.dma_start(wup[RANK:RANK + 1, :], gla_b_up).then_inc(small_in, 16)
            act.dma_start(gate_w[:, 0], rg_wa[0].rearrange("j p n -> p j n")).then_inc(gates_in, 16)
            act.dma_start(gate_w[:, 1], rg_wx[0].rearrange("j p n -> p j n")).then_inc(gates_in, 16)
            act.wait_ge(small_in, 16 * SMALL)
            act.activation(c_col[:], c_col[:], ACT.Silu).then_inc(c_ready, 1)
            act.wait_ge(x_in, 16)
            for t in range(TT):
                if t:
                    act.wait_ge(sums1, t)
                act.activation(tmp_tok[:, 0], x_tok[:, t], ACT.Square, accum_out=stat[:, t:t + 1]).then_inc(sums1, 1)
            act.wait_ge(sums1, TT)
            act.wait_ge(consts_ready, 1)
            act.activation(rstd[:, 0:TT], stat[:, 0:TT], ACT.Sqrt, bias=eps[:], scale=1.0 / D).then_inc(roots1, 1)
            for t in range(TT):
                for g in range(2):
                    wait_job(act, ("uT", t, g))
                    act.activation(uT[:, 4 * g:4 * g + 4, t * P:(t + 1) * P], bank(("uT", t, g)).rearrange("p (k n) -> p k n", k=4), ACT.Copy).then_inc(act_emptied, 1)
            wait_job(act, "lr")
            act.activation(lrT[0:RANK, :], bank("lr")[0:RANK, :], ACT.Copy).then_inc(act_emptied, 1)
            for t in range(TT):
                wait_emptied(act, ("gate", t))
                own(act.activation(er[:, t], la[:, t], ACT.Abs))
                own.settle()
                own(act.activation(er[:, t], er[:, t], ACT.Exp, scale=-1.0))
                own.settle()
                act.activation(er[:, t], er[:, t], ACT.Ln, bias=1.0).then_inc(log_ready, 1)
            wait_emptied(act, "vectors")
            own(act.activation(sp4[:, 0:8], vec[:, LAM:LAM + 8], ACT.Abs))
            own.settle()
            own(act.activation(sp4[:, 0:8], sp4[:, 0:8], ACT.Exp, scale=-1.0))
            own.settle()
            act.activation(sp4[:, 0:8], sp4[:, 0:8], ACT.Ln, bias=1.0).then_inc(sp_ready, 1)
            for n in range(2):
                for t in range(TT):
                    wait_job(act, ("v", n, t))
                    act.activation(v_tok[:, t, n * NC:(n + 1) * NC], bank(("v", n, t)), ACT.Copy).then_inc(act_emptied, 1)
            for t in range(TT):
                act.wait_ge(la_ready, t + 1)
                wait_job(act, ("rem", t))
                act.activation(er[:, t], bank(("rem", t)), ACT.Exp, scale=1.0 / 16).then_inc(act_emptied, 1)
            wait_job(act, "tot")
            act.activation(decay[:], bank("tot")[:, 0:HEADS * NCHUNK].rearrange("p (h n) -> p h n", h=HEADS), ACT.Exp, scale=1.0 / 16).then_inc(act_emptied, 1)
            for h in range(HEADS):
                wait_job(act, ("q", h))
                act.activation(qT[:, h], bank(("q", h)), ACT.Copy, scale=DK ** -0.5).then_inc(act_emptied, 1)
            for n in range(NCHUNK):
                wait_job(act, ("o", n))
                act.activation(oT[:, :, n * CHUNK:(n + 1) * CHUNK], bank(("o", n)).rearrange("p (k n) -> p k n", k=KT), ACT.Copy).then_inc(act_emptied, 1)
            for j in range(KT):
                wait_job(act, ("rg", j))
                act.activation(hgT[:, j], bank(("rg", j)), ACT.Gelu_apprx_tanh).then_inc(act_emptied, 1)
            wait_emptied(act, ("o", NCHUNK - 1))
            for h in range(HEADS):
                if h >= 2:
                    wait_job(act, ("ss", h - 2))
                act.activation(tmpT[:, 2 * (h % 2):2 * (h % 2) + 2], oT[:, 2 * h:2 * h + 2], ACT.Square).then_inc(sq_ready, 1)
            for h in range(HEADS):
                wait_job(act, ("ss", h))
                if h == 0:
                    wait_emptied(act, ("q", HEADS - 1))
                    wait_job(act, ("kv", NCHUNK - 1, 1))
                act.activation(la[:, h], bank(("ss", h)), ACT.Sqrt, bias=eps[:], scale=1.0 / DV).then_inc(act_emptied, 1)
            for j in range(KT):
                wait_job(act, ("og", j))
                if j >= 4:
                    act.wait_ge(og_used, j - 3)
                if j < 4:
                    wait_job(act, ("ss", HEADS - 1))
                act.activation(tmpT[:, j % 4], bank(("og", j)), ACT.Silu).then_inc(act_emptied, 1)
            for n in range(2):
                for q in range(4):
                    j = 4 * n + q
                    wait_job(act, ("ra", j))
                    act.wait_ge(rg_done, 4 * n)
                    act.wait_ge(sp_ready, 2)
                    own(act.activation(tau[:, q], bank(("ra", j)), ACT.Sigmoid, bias=vec[:, BA + j:BA + j + 1]))
                    own.settle()
                    act.activation(tau[:, q], tau[:, q], ACT.Tanh, scale=sp4[:, 8 + j:9 + j]).then_inc(act_emptied, 1)
                    wait_job(act, ("ri", j))
                    if n == 0:
                        act.wait_ge(og_used, KT)
                    act.activation(tmpT[:, q], bank(("ri", j)), ACT.Sigmoid, bias=vec[:, BX + j:BX + j + 1]).then_inc(act_emptied, 1)
                for q in range(4):
                    j = 4 * n + q
                    act.wait_ge(ri_ready, j + 1)
                    wait_emptied(act, ("ra", j))
                    act.activation(tmpT[:, q], tau[:, q], ACT.Sqrt).then_inc(sqrt_ready, 1)
            for gate, y in (("gb", "yb"), ("ga", "ya")):
                for j in range(KT):
                    wait_job(act, (gate, j))
                    if gate == "gb" and j < 4:
                        act.wait_ge(rg_done, KT)
                    elif j >= 4:
                        wait_emptied(act, (y, j - 4))
                    else:
                        wait_emptied(act, ("yb", j + 4))
                    act.activation(tmpT[:, j % 4], bank((gate, j)), ACT.Sigmoid).then_inc(act_emptied, 1)
            act.dma_start(row_a[:], norm2_g.broadcast_to([P, D])).then_inc(n2_in, 16)
            act.wait_ge(h_res, TT)
            act.dma_start(router[:], k_major(router_w[0])).then_inc(router_in, 16)
            act.dma_start(bias_row[:], router_b.broadcast_to([P, E])).then_inc(router_in, 16)
            for t in range(TT):
                act.wait_ge(h_res, TT + t + 1)
                act.activation(xT[:].rearrange("p k n -> p (k n)"), x_tok[:, t], ACT.Square, accum_out=stat[:, 4 + t:5 + t]).then_inc(sums2, 1)
                act.wait_ge(sums2, t + 1)
                act.activation(rstd[:, 4 + t:5 + t], stat[:, 4 + t:5 + t], ACT.Sqrt, bias=eps[:], scale=1.0 / D).then_inc(roots2, 1)
            for t in range(TT):
                act.wait_ge(u2_ready, t + 1)
                act.dma_start(u2_dram.rearrange("(t p) d -> p t d", p=P)[:, t], tmp_tok[:, t % 2]).then_inc(u2_out[t % 2], 16)
                for g in range(2):
                    wait_job(act, ("u2T", t, g))
                    act.activation(u2T[:, 4 * g:4 * g + 4, t * P:(t + 1) * P], bank(("u2T", t, g)).rearrange("p (k n) -> p k n", k=4), ACT.Copy).then_inc(act_emptied, 1)
            for t in range(TT):
                wait_job(act, ("router", t))
                act.activation(scores[:, t], bank(("router", t))[:, 0:E], ACT.Sigmoid).then_inc(act_emptied, 1)
            act.dma_start(row_a[:], final_g.rearrange("(o d) -> o d", o=1).broadcast_to([P, D])).then_inc(fg_in, 16)
            for t in range(TT):
                wait_job(act, ("sgu", t))
                if t:
                    wait_emptied(act, ("sgu", t - 1))
                act.activation(sgate, bank(("sgu", t))[:, 0:DE], ACT.Silu).then_inc(sgate_ready, 1)
            for t in range(TT):
                wait_job(act, ("shT", t))
                act.activation(shT[:, :, t * P:(t + 1) * P], bank(("shT", t))[:, 0:2 * P].rearrange("p (j n) -> p j n", j=2), ACT.Copy).then_inc(act_emptied, 1)
            for n in range(2):
                for t in range(TT):
                    wait_job(act, ("sdown", n, t))
                    act.activation(sum_tok[:, t, n * NC:(n + 1) * NC], bank(("sdown", n, t)), ACT.Copy).then_inc(act_emptied, 1)
            wait_emptied(act, ("sdown", 1, TT - 1))
            act.dma_start(sum_dram[0:T].rearrange("(t p) d -> p t d", p=P), sum_tok).then_inc(sum_started, 16)

            def turned_rows(n):
                for g in range(2):
                    act.wait_ge(xT_psum, 2 * n + 1 + g)
                    act.activation(xT[:, 4 * g:4 * g + 4], moe_bank(g).rearrange("p (k n) -> p k n", k=4), ACT.Copy).then_inc(xT_ready, 1)

            turned_rows(0)
            act.wait_ge(tables_ready, 1)
            act.nop().then_inc(y_ready, 2)
            for i, s, b in live_blocks(act):
                act.wait_ge(gu_done, b + 1)
                act.wait_ge(h_ready, b + 1)
                act.activation(gate_h, moe_bank(GU)[:, 0:DE], ACT.Silu).then_inc(silu_done, 1)
                turned_rows(b + 1)
                act.wait_ge(idx_ready, b + 1)
                act.wait_ge(scattered, 16 * b + 16)
                for g in range(2):
                    act.wait_ge(y_psum, 2 * b + 3 + g)
                    act.activation(y_rows[:, g * NC:(g + 1) * NC], moe_bank(Y0 + g), ACT.Copy, scale=row_w[:, s:s + 1]).then_inc(y_ready, 1)
            for t in range(TT):
                act.wait_ge(h2_res, t + 1)
                act.activation(xT[:].rearrange("p k n -> p (k n)"), x_tok[:, t], ACT.Square, accum_out=stat[:, t:t + 1]).then_inc(sums3, 1)
                act.wait_ge(sums3, t + 1)
                act.activation(rstd[:, t:t + 1], stat[:, t:t + 1], ACT.Sqrt, bias=eps[:], scale=1.0 / D).then_inc(roots3, 1)

        @block.vector
        def _(dve):
            own = Own(dve, dve_own)
            tt, ts, stt = dve.tensor_tensor, dve.tensor_scalar, dve.scalar_tensor_tensor
            wait_job(dve, "vectors")
            dve.tensor_copy(vec[:], bank("vectors")[:, 0:72]).then_inc(dve_emptied, 1)
            dve.wait_ge(small_in, 16 * SMALL)
            for n in range(4):
                wait_job(dve, ("ada", n))
                tt(sh1sc1[:, n], bank(("ada", n)), sh1sc1[:, n], ALU.add).then_inc(dve_emptied, 1)
            wait_emptied(dve, ("ada", 3))
            own(stt(row_a[:], sh1sc1[:, 2:4].rearrange("p a n -> p (a n)"), 1.0, row_a[:], ALU.add, ALU.mult))
            dve.wait_ge(roots1, 1)
            own(dve.reciprocal(rstd[:, 0:TT], rstd[:, 0:TT]))
            own.settle()
            for t in range(TT):
                if t >= 2:
                    wait_job(dve, ("uT", t - 2, 1))
                own(stt(tmp_tok[:, t % 2], x_tok[:, t], rstd[:, t:t + 1], row_a[:], ALU.mult, ALU.mult))
                own.settle()
                tt(tmp_tok[:, t % 2], tmp_tok[:, t % 2], sh1sc1[:, 0:2].rearrange("p a n -> p (a n)"), ALU.add).then_inc(u_ready, 1)
            dve.wait_ge(u_ready, TT)
            for t in range(TT):
                wait_job(dve, ("gate", t))
                dve.tensor_copy(la[:, t], bank(("gate", t))).then_inc(dve_emptied, 1)
            for t in range(TT):
                dve.wait_ge(log_ready, t + 1)
                stt(la[:, t], la[:, t], 0.0, er[:, t], ALU.min, ALU.subtract).then_inc(la_ready, 1)
            dve.wait_ge(sp_ready, 1)
            own(stt(sp4[:, 0:8], vec[:, LAM:LAM + 8], 0.0, sp4[:, 0:8], ALU.min, ALU.subtract))
            own.settle()
            ts(sp4[:, 8:16], sp4[:, 0:8], -RG_C / 2, None, ALU.mult).then_inc(sp_ready, 1)
            for t in range(TT):
                wait_job(dve, ("k", t))
                wait_emptied(dve, ("rem", t))
                tt(er[:, t], bank(("k", t)), er[:, t], ALU.mult).then_inc(dve_emptied, 1)
            wait_emptied(dve, "tot")
            for n in range(NCHUNK):
                if n >= 2:
                    wait_job(dve, ("o", n - 2))
                if n >= 1:
                    wait_emptied(dve, ("kv", n - 1, 1))
                for g in range(2):
                    wait_job(dve, ("kv", n, g))
                    for h in range(2 * g, 2 * g + 2):
                        kv = bank(("kv", n, g))[:, (h % 2) * DV:(h % 2 + 1) * DV]
                        if n == 0:
                            ins = dve.tensor_copy(state[:, 0, h], kv)
                        else:
                            ins = stt(state[:, n % 2, h], state[:, (n - 1) % 2, h], decay[:, h, n:n + 1], kv, ALU.mult, ALU.add)
                        if h % 2 == 0:
                            own(ins)
                    ins.then_inc(dve_emptied, 1)
            for j in range(KT):
                h = j // 2
                if j % 2 == 0:
                    wait_emptied(dve, ("ss", h))
                    own(dve.reciprocal(la[:, h], la[:, h]))
                    own.settle()
                dve.wait_ge(sq_ready, h + 1)
                own(stt(oT[:, j], oT[:, j], vec[:, GN + j:GN + j + 1], la[:, h], ALU.mult, ALU.mult))
                own.settle()
                wait_emptied(dve, ("og", j))
                tt(oT[:, j], oT[:, j], tmpT[:, j % 4], ALU.mult).then_inc(og_used, 1)
            for n in range(2):
                for q in range(4):
                    j = 4 * n + q
                    wait_job(dve, ("rx", j))
                    rx = bank(("rx", j))
                    tap = lambda d: vec[:, CW + 8 * (CONV_W - 1 - d) + j:CW + 8 * (CONV_W - 1 - d) + j + 1]
                    own(ts(xr[:, q], rx, tap(0), vec[:, CB + j:CB + j + 1], ALU.mult, ALU.add))
                    for d in range(1, CONV_W):
                        own.settle()
                        ins = stt(xr[:, q, d:T], rx[:, 0:T - d], tap(d), xr[:, q, d:T], ALU.mult, ALU.add)
                        if d < CONV_W - 1:
                            own(ins)
                    ins.then_inc(dve_emptied, 1)
                for q in range(4):
                    j = 4 * n + q
                    wait_emptied(dve, ("ri", j))
                    tt(xr[:, q], xr[:, q], tmpT[:, q], ALU.mult).then_inc(ri_ready, 1)
                dve.wait_ge(ri_ready, 4 * n + 4)
                for q in range(4):
                    j = 4 * n + q
                    dve.wait_ge(sqrt_ready, j + 1)
                    own(ts(t1, tau[:, q], 1.0, None, ALU.add))
                    own.settle()
                    own(dve.reciprocal(t1, t1))
                    own.settle()
                    own(stt(t2, tmpT[:, q], 2.0, t1, ALU.mult, ALU.mult))
                    own(ts(tau[:, q], t1, 2.0, -1.0, ALU.mult, ALU.add))
                    own.settle()
                    own(dve.memset(t2[:, 0:1], 1.0))
                    own.settle()
                    own(tt(xr[:, q], xr[:, q], t2, ALU.mult))
                    own.settle()
                    own(dve.tensor_tensor_scan(t2, tau[:, q], xr[:, q], 0.0, ALU.mult, ALU.add))
                    own.settle()
                    tt(hgT[:, j], hgT[:, j], t2, ALU.mult).then_inc(rg_done, 1)
                for i in range(4 + 4 * n, 8 + 4 * n):
                    wait_job(dve, ("ada", i))
                    tt(mods[:, i - 4], bank(("ada", i)), mods[:, i - 4], ALU.add).then_inc(dve_emptied, 1)
            for j in range(KT):
                wait_emptied(dve, ("gb", j))
                wait_job(dve, ("yb", j))
                tt(mT[:, j], bank(("yb", j)), tmpT[:, j % 4], ALU.mult).then_inc(dve_emptied, 1)
            for j in range(KT):
                wait_emptied(dve, ("ga", j))
                wait_job(dve, ("ya", j))
                if j:
                    dve.wait_ge(m_ready, j)
                tt(t1, bank(("ya", j)), tmpT[:, j % 4], ALU.mult).then_inc(dve_emptied, 1)
                wait_emptied(dve, ("ya", j))
                tt(mT[:, j], mT[:, j], t1, ALU.add).then_inc(m_ready, 1)
            for n in range(2):
                for t in range(TT):
                    wait_job(dve, ("out", n, t))
                    if n or t:
                        dve.wait_ge(h_res, TT * n + t)
                    tt(t1, bank(("out", n, t)), mods[:, n], ALU.mult).then_inc(dve_emptied, 1)
                    wait_emptied(dve, ("out", n, t))
                    tt(x_tok[:, t, n * NC:(n + 1) * NC], x_tok[:, t, n * NC:(n + 1) * NC], t1, ALU.add).then_inc(h_res, 1)
            dve.wait_ge(n2_in, 16)
            own(stt(row_a[:], mods[:, 4:6].rearrange("p a n -> p (a n)"), 1.0, row_a[:], ALU.add, ALU.mult))
            own.settle()
            for t in range(TT):
                dve.wait_ge(roots2, t + 1)
                own(dve.reciprocal(rstd[:, 4 + t:5 + t], rstd[:, 4 + t:5 + t]))
                own.settle()
                if t >= 2:
                    wait_job(dve, ("u2T", t - 2, 1))
                    dve.wait_ge(u2_out[t % 2], 16 * (t // 2))
                own(stt(tmp_tok[:, t % 2], x_tok[:, t], rstd[:, 4 + t:5 + t], row_a[:], ALU.mult, ALU.mult))
                own.settle()
                tt(tmp_tok[:, t % 2], tmp_tok[:, t % 2], mods[:, 2:4].rearrange("p a n -> p (a n)"), ALU.add).then_inc(u2_ready, 1)
            dve.wait_ge(router_in, 32)
            for t in range(TT):
                wait_emptied(dve, ("router", t))
                own(tt(sel[:, t], scores[:, t], bias_row[:], ALU.add))
                own.settle()
                own(dve.max(top8[:, t], sel[:, t]))
                own.settle()
                own(dve.match_replace(slot[:, t], top8[:, t], sel[:, t], -3e38))
                own.settle()
                own(tt(mask[:, t], slot[:, t], sel[:, t], ALU.not_equal))
                own.settle()
                dve.tensor_copy(mask_b[:, t], mask[:, t]).then_inc(mask_ready, 1)
                own(tt(w_left[:, t], scores[:, t], mask[:, t], ALU.mult))
                own.settle()
                own(dve.tensor_reduce(got[:, t:t + 1], w_left[:, t], AX_X, ALU.add))
                own.settle()
                own(dve.reciprocal(got[:, t:t + 1], got[:, t:t + 1]))
                own.settle()
                own(ts(w_left[:, t], w_left[:, t], got[:, t:t + 1], ROUTED_SCALE, ALU.mult, ALU.mult))
                own.settle()
            for i in range(3):
                own(dve.tensor_copy(w3[:, :, :, i], w_left[:]))
                own.settle()
                if i < 2:
                    own(tt(w_left[:], w_left[:], w3[:, :, :, i], ALU.subtract))
                    own.settle()
            for t in range(TT):
                wait_job(dve, ("sgu", t))
                dve.wait_ge(sgate_ready, t + 1)
                tt(sh_tok[:, t], sgate, bank(("sgu", t))[:, DE:2 * DE], ALU.mult).then_inc(dve_emptied, 1)
            wait_job(dve, "count")
            dve.tensor_copy(n_col[:, 0:1], bank("count")[:, 0:1]).then_inc(dve_emptied, 1)
            wait_emptied(dve, "count")
            own(ts(n_col[:, 4:8], block_start[:, 0:TT], n_col[:, 0:1], None, ALU.is_lt))
            own.settle()
            own(dve.tensor_reduce(n_col[:, 1:2], n_col[:, 4:8], AX_X, ALU.add))
            own.settle()
            ts(nb_rep[:], ones_b[:], n_col[:, 1:2], None, ALU.mult).then_inc(nb_ready, 1)
            wait_job(dve, "pos")
            dve.tensor_copy(slot[:].rearrange("p t e -> p (t e)"), bank("pos")).then_inc(dve_emptied, 1)
            wait_job(dve, "bstart_col")
            tt(n_col[:, 3:4], bank("bstart_col")[:, 0:1], n_col[:, 1:2], ALU.add).then_inc(dve_emptied, 1)
            wait_emptied(dve, "bstart_col")
            own(ts(n_col[:, 3:4], n_col[:, 3:4], float(P), None, ALU.mult))
            own.settle()
            wait_job(dve, "bstart_row")
            ts(sel[:, 0], bank("bstart_row")[:, 0:E], float(P), 1.0, ALU.mult, ALU.add).then_inc(dve_emptied, 1)
            wait_emptied(dve, "bstart_row")
            ts(over[:], block_start[:], n_col[:, 3:4], None, ALU.is_ge).then_inc(over_ready, 1)
            for t in range(TT):
                own(tt(slot[:, t], slot[:, t], sel[:, 0], ALU.add))
            own.settle()
            own(tt(slot[:], slot[:], mask[:], ALU.mult))
            own.settle()
            own(ts(slot[:], slot[:], -1.0, None, ALU.add))
            wait_job(dve, "table")
            own(ts(live_row, bank("table")[0:1, 0:TABLE], float(E), None, ALU.is_lt))
            own.settle()
            own(dve.tensor_reduce(n_col[0:1, 2:3], live_row, AX_X, ALU.add))
            own.settle()
            own(dve.tensor_copy(live_count[:], n_col[0:1, 2:3]))
            own(ts(live_of[0:1, :], bank("table")[0:1, 0:TABLE], float(E), None, ALU.is_lt))
            ts(expert_of[0:1, :], bank("table")[0:1, 0:TABLE], float(E - 1), None, ALU.min).then_inc(dve_emptied, 1)
            wait_emptied(dve, "table")
            dve.wait_ge(xg_zero, 2)
            own(dve.tensor_copy(pick_cols[:, :, 0:2], tok_cols[:]))
            own.settle()
            dve.nop().then_inc(tables_ready, 1)

            def pick_rows(n):
                e = dve.value_load(expert_of[0:1, bass.ds(n, 1)], min_val=0, max_val=E - 1)
                if not isinstance(n, int) or n:
                    dve.wait_ge(idx_psum, n)
                for t in range(TT):
                    own_loop = ts(pick[:, t], iota_row[:], block_start[:, bass.ds(n, 1)], slot[:, t, bass.ds(e, 1)], ALU.add, ALU.is_equal)
                    own_loop.then_inc(pick_ready, 1)
                dve.tensor_copy(pick_cols[:, :, 2:5], w3[:, :, bass.ds(e, 1), :].rearrange("p t o w -> p t (o w)")).then_inc(pick_ready, 1)

            def find_rows(n, s):
                dve.wait_ge(idx_psum, n + 1)
                dve.tensor_copy(got[:, 0:5], moe_bank(IDX)[:, 0:5]).then_inc(found, 1)
                dve.wait_ge(found, 4 * n + 1)
                stt(got[:, 5:6], got[:, 0:1], -1.0, got[:, 1:2], ALU.add, ALU.add).then_inc(found, 1)
                dve.wait_ge(found, 4 * n + 2)
                stt(got[:, 6:7], got[:, 5:6], 0.0, dummy_row[:], ALU.is_lt, ALU.mult).then_inc(found, 1)
                stt(row_w[:, s:s + 1], got[:, 2:3], got[:, 3:4], got[:, 4:5], ALU.add, ALU.add).then_inc(found, 1)
                dve.wait_ge(found, 4 * n + 4)
                tt(row_idx[:, s], got[:, 5:6], got[:, 6:7], ALU.add).then_inc(idx_ready, 1)

            dve.nop().then_inc(h_ready, 1)
            for n in range(2):
                pick_rows(n)
                find_rows(n, n)
            for i, s, b in live_blocks(dve):
                dve.wait_ge(silu_done, b + 1)
                dve.wait_ge(hT_psum, b + 1)
                tt(h_tok, gate_h, moe_bank(GU)[:, DE:2 * DE], ALU.mult).then_inc(h_ready, 1)
                pick_rows(b + 2)
                dve.wait_ge(hT_psum, b + 2)
                dve.wait_ge(y_psum, 2 * b + 2)
                dve.tensor_copy(hT, moe_bank(HT)[:, 0:2 * P].rearrange("p (j n) -> p j n", j=2)).then_inc(hT_ready, 1)
                dve.wait_ge(y_ready, 2 * b + 2)
                dve.tensor_copy(add_idx[:, s], row_idx[:, s]).then_inc(add_ready, 1)
                find_rows(b + 2, (s + 2) % UNROLL)
            dve.wait_ge(sum_in, 16)
            for t in range(TT):
                own2 = tt(sum_tok[:, t], sum_tok[:, t], g2_row, ALU.mult)
                own(own2)
                own.settle()
                tt(x_tok[:, t], x_tok[:, t], sum_tok[:, t], ALU.add).then_inc(h2_res, 1)
            dve.wait_ge(fg_in, 16)
            for t in range(TT):
                dve.wait_ge(roots3, t + 1)
                own(dve.reciprocal(rstd[:, t:t + 1], rstd[:, t:t + 1]))
                own.settle()
                stt(x_tok[:, t], x_tok[:, t], rstd[:, t:t + 1], row_a[:], ALU.mult, ALU.mult).then_inc(out_ready, 1)

        @block.tensor
        def _(pe):
            def start_job(name):
                n = J[name]
                if n >= BANKS:
                    wait_emptied(pe, jobs[n - BANKS][0])

            def end_job(ins):
                ins.then_inc(job_done, 1)

            def product(name, lhs, rhs, dst=None, tiles=KT):
                start_job(name)
                dst = bank(name) if dst is None else dst
                for k in range(tiles):
                    mm = pe.matmul(dst, lhs(k), rhs(k), start=(k == 0), stop=(k == tiles - 1))
                end_job(mm)

            def turn(name, src, tiles):
                start_job(name)
                for i, k in enumerate(tiles):
                    mm = pe.transpose(bank(name)[:, i * P:(i + 1) * P], src(k), ident[:])
                end_job(mm)

            def feature_major(name, j, weights, acts):
                product(name, lambda k: weights[:, k, (j % 4) * P:(j % 4 + 1) * P], lambda k: acts[:, k])

            def token_major(name, t, weights, acts, tiles=KT):
                product(name, lambda k: acts[:, k, t * P:(t + 1) * P], lambda k: weights[:, k], tiles=tiles)

            pe.wait_ge(consts_ready, 1)
            pe.wait_ge(rows_in, 16 * 6)
            start_job("vectors")
            end_job(pe.transpose(bank("vectors")[:, 0:72], vec_rows, ident[0:72, 0:72]))
            pe.wait_ge(c_rep_ready, 1)

            def ada(i):
                wait_chunk(pe, ("ada", i))
                product(("ada", i), lambda k: c_rep[:, k], lambda k: chunk(("ada", i))[:, k])

            for i in range(4):
                ada(i)
            for t in range(TT):
                pe.wait_ge(u_ready, t + 1)
                for g in range(2):
                    turn(("uT", t, g), lambda k: tmp_tok[:, t % 2, k * P:(k + 1) * P], range(4 * g, 4 * g + 4))
            wait_emptied(pe, ("uT", TT - 1, 1))
            product("lr", lambda k: wlr[:, k], lambda k: uT[:, k], dst=bank("lr")[0:RANK, :])
            wait_emptied(pe, "lr")
            for t in range(TT):
                product(("gate", t), lambda k: lrT[0:RANK + 1, t * P:(t + 1) * P], lambda k: wup[0:RANK + 1, :], tiles=1)
            for n in range(2):
                wait_chunk(pe, ("v", n))
                for t in range(TT):
                    token_major(("v", n, t), t, chunk(("v", n)), uT)
            for t in range(TT):
                pe.wait_ge(la_ready, t + 1)
                product(("rem", t), lambda k: later[:], lambda k: la[:, t], tiles=1)
            start_job("tot")
            for h in range(HEADS):
                for t in range(TT):
                    at = h * NCHUNK + 2 * t
                    mm = pe.matmul(bank("tot")[:, at:at + 2], la[:, t, h * DK:(h + 1) * DK], in_chunk[:], start=True, stop=True)
            end_job(mm)
            wait_chunk(pe, "k")
            for t in range(TT):
                token_major(("k", t), t, chunk("k"), uT)
            wait_chunk(pe, "q")
            for h in range(HEADS):
                feature_major(("q", h), h, chunk("q"), uT)
            for n in range(NCHUNK + 1):
                if n < NCHUNK:
                    t, lo = n // 2, (n % 2) * CHUNK
                    wait_emptied(pe, ("k", t))
                    for g in range(2):
                        start_job(("kv", n, g))
                        for h in range(2 * g, 2 * g + 2):
                            mm = pe.matmul(bank(("kv", n, g))[:, (h % 2) * DV:(h % 2 + 1) * DV], er[lo:lo + CHUNK, t, h * DK:(h + 1) * DK],
                                           v_tok[lo:lo + CHUNK, t, h * DV:(h + 1) * DV], start=True, stop=True)
                        end_job(mm)
                if n >= 1:
                    m = n - 1
                    wait_emptied(pe, ("kv", m, 1))
                    wait_emptied(pe, ("q", HEADS - 1))
                    start_job(("o", m))
                    for j in range(KT):
                        mm = pe.matmul(bank(("o", m))[:, j * CHUNK:(j + 1) * CHUNK], state[:, m % 2, j // 2, (j % 2) * P:(j % 2 + 1) * P],
                                       qT[:, j // 2, m * CHUNK:(m + 1) * CHUNK], start=True, stop=True)
                    end_job(mm)
            for j in range(KT):
                if j % 4 == 0:
                    wait_chunk(pe, ("rg", j // 4))
                feature_major(("rg", j), j, chunk(("rg", j // 4)), uT)
            for h in range(HEADS):
                pe.wait_ge(sq_ready, h + 1)
                product(("ss", h), lambda k: ones[:], lambda k: tmpT[:, 2 * (h % 2) + k], tiles=2)
            for j in range(KT):
                if j % 4 == 0:
                    wait_chunk(pe, ("og", j // 4))
                feature_major(("og", j), j, chunk(("og", j // 4)), uT)
            pe.wait_ge(gates_in, 32)
            for n in range(2):
                wait_chunk(pe, ("rx", n))
                for j in range(4 * n, 4 * n + 4):
                    feature_major(("rx", j), j, chunk(("rx", n)), uT)
                for j in range(4 * n, 4 * n + 4):
                    wait_emptied(pe, ("rx", j))
                    for i, name in enumerate(("ra", "ri")):
                        product((name, j), lambda k: gate_w[:, i, j], lambda k: xr[:, j % 4], tiles=1)
                for i in range(4 + 4 * n, 8 + 4 * n):
                    ada(i)
            for gate, y, acts in (("gb", "yb", oT), ("ga", "ya", hgT)):
                if gate == "gb":
                    pe.wait_ge(og_used, KT)
                else:
                    pe.wait_ge(rg_done, KT)
                for n in range(2):
                    wait_chunk(pe, (gate, n))
                    for j in range(4 * n, 4 * n + 4):
                        feature_major((gate, j), j, chunk((gate, n)), uT)
                    wait_chunk(pe, (y, n))
                    for j in range(4 * n, 4 * n + 4):
                        feature_major((y, j), j, chunk((y, n)), acts)
            pe.wait_ge(m_ready, KT)
            for n in range(2):
                wait_chunk(pe, ("out", n))
                for t in range(TT):
                    token_major(("out", n, t), t, chunk(("out", n)), mT)
            for t in range(TT):
                pe.wait_ge(u2_ready, t + 1)
                for g in range(2):
                    turn(("u2T", t, g), lambda k: tmp_tok[:, t % 2, k * P:(k + 1) * P], range(4 * g, 4 * g + 4))
            pe.wait_ge(router_in, 32)
            for t in range(TT):
                wait_emptied(pe, ("u2T", t, 1))
                product(("router", t), lambda k: u2T[:, k, t * P:(t + 1) * P], lambda k: router[:, k], dst=bank(("router", t))[:, 0:E])
            wait_chunk(pe, "sgu")
            for t in range(TT):
                token_major(("sgu", t), t, chunk("sgu"), u2T)
            pe.wait_ge(mask_ready, TT)
            product("count", lambda t: mask_b[:, t], lambda t: ones_b[:, 0:1], dst=bank("count")[:, 0:1], tiles=TT)
            start_job("pos")
            for t in range(TT):
                for i in range(t + 1):
                    mm = pe.matmul(bank("pos")[:, t * E:(t + 1) * E], tri[:] if i == t else ones_b[:], mask_b[:, i], start=(i == 0), stop=(i == t))
            end_job(mm)
            pe.wait_ge(nb_ready, 1)
            product("bstart_col", lambda k: tri[:], lambda k: nb_rep[:, 0:1], dst=bank("bstart_col")[:, 0:1], tiles=1)
            product("bstart_row", lambda k: nb_rep[:], lambda k: tri[:], dst=bank("bstart_row")[:, 0:E], tiles=1)
            pe.wait_ge(over_ready, 1)
            product("table", lambda k: ones_b[:, 0:1], lambda k: over[:], dst=bank("table")[0:1, 0:TABLE], tiles=1)
            for t in range(TT):
                wait_emptied(pe, ("sgu", t))
                turn(("shT", t), lambda k: sh_tok[:, t, k * P:(k + 1) * P], range(2))
            wait_chunk(pe, "sdown")
            wait_emptied(pe, ("shT", TT - 1))
            for n in range(2):
                for t in range(TT):
                    product(("sdown", n, t), lambda k: shT[:, k, t * P:(t + 1) * P], lambda k: sdown_w[:, k, n * NC:(n + 1) * NC], tiles=2)

            def find(n):
                pe.wait_ge(pick_ready, 5 * n + 5)
                if not isinstance(n, int) or n:
                    pe.wait_ge(idx_ready, n)
                for t in range(TT):
                    mm = pe.matmul(moe_bank(IDX)[:, 0:5], pick[:, t], pick_cols[:, t], start=(t == 0), stop=(t == TT - 1))
                mm.then_inc(idx_psum, 1)

            def turn_rows(n, s, uses):
                pe.wait_ge(gathered[s], uses)
                for k in range(KT):
                    mm = pe.transpose(moe_bank(k // 4)[:, (k % 4) * P:(k % 4 + 1) * P], xg[:, s, bass.ds(k, P, KT)], ident[:])
                    if k % 4 == 3:
                        mm.then_inc(xT_psum, 1)

            pe.wait_ge(act_emptied, emptied_by.count("act"))
            pe.wait_ge(dve_emptied, emptied_by.count("dve"))
            pe.wait_ge(tables_ready, 1)
            pe.nop().then_inc(hT_psum, 1)
            pe.nop().then_inc(y_psum, 2)
            find(0)
            find(1)
            turn_rows(0, 0, 16)
            for i, s, b in live_blocks(pe):
                pe.wait_ge(w_loaded[s], 32 * i + 32)
                pe.wait_ge(xT_ready, 2 * b + 2)
                for k in range(KT):
                    mm = pe.matmul(moe_bank(GU), xT[:, k], w_gu[:, s, k], start=(k == 0), stop=(k == KT - 1))
                mm.then_inc(gu_done, 1)
                turn_rows(b + 1, (s + 1) % UNROLL, 16 * i + 16 + 16 * ((s + 1) // UNROLL))
                pe.wait_ge(h_ready, b + 2)
                for j in range(2):
                    mm = pe.transpose(moe_bank(HT)[:, j * P:(j + 1) * P], h_tok[:, j * P:(j + 1) * P], ident[:])
                mm.then_inc(hT_psum, 1)
                find(b + 2)
                pe.wait_ge(hT_ready, b + 1)
                pe.wait_ge(y_ready, 2 * b + 2)
                for g in range(2):
                    for j in range(2):
                        mm = pe.matmul(moe_bank(Y0 + g), hT[:, j], w_dn[:, s, j, g * NC:(g + 1) * NC], start=(j == 0), stop=(j == 1))
                    mm.then_inc(y_psum, 1)



_INS = ["x", "c", "ada_w", "ada_b", "norm1_g", "w_in", "conv_w", "conv_b", "rg_wa", "rg_ba", "rg_wx", "rg_bx",
        "rg_lambda", "gla_w_up", "gla_b_up", "gla_norm_g", "w_branch_a", "w_branch_b", "w_out", "norm2_g",
        "router_w", "router_b", "exp_w_gu", "exp_w_down", "shared_w_gu", "shared_w_down", "final_g"]


def kernel(**inputs):
    import numpy as _np
    import concourse.bacc as _bacc
    from concourse import mybir as _mybir
    from concourse.bass_utils import run_bass_kernel_spmd as _run

    nc = _bacc.Bacc("TRN2", target_bir_lowering=False, num_devices=1)
    arrays, args = {}, []
    for name in _INS:
        a = _np.ascontiguousarray(inputs[name])
        arrays[f"in_{name}"] = a
        args.append(nc.dram_tensor(f"in_{name}", a.shape, _mybir.dt.from_np(a.dtype), kind="ExternalInput").ap())
    result = nc.dram_tensor("result", (1, T, D), _mybir.dt.float32, kind="ExternalOutput").ap()
    layer_program(nc, *args, result)
    r = _run(nc, [arrays], core_ids=[0])
    return r.results[0]["result"]
```

```python
from contextlib import ExitStack

import concourse.bass as bass
from concourse import mybir

ALU = mybir.AluOpType
ACT = mybir.ActivationFunctionType
F32 = mybir.dt.float32
F32R = mybir.dt.float32r
BF16 = mybir.dt.bfloat16
U32 = mybir.dt.uint32
AX_X = mybir.AxisListType.X

P = 128
T = 512
TT = T // P
D = 1024
KT = D // P
NC = 512
CHUNK = 64
NCHUNK = T // CHUNK
HEADS = 4
DK = 128
DV = 256
RANK = 16
RNN_BLOCKS = 8
CONV_W = 4
RG_C = 8.0
EPS = 1e-6
E = 128
TOP_K = 8
DE = 256
MOE_BLOCKS = (T * TOP_K - E) // P + E
UNROLL, SPAN = 3, 6
SPANS = -(-MOE_BLOCKS // (UNROLL * SPAN))
TABLE = SPANS * SPAN * UNROLL + UNROLL
ROUTED_SCALE = 2.5
BANKS = 8

W_RX, W_RG, W_Q, W_K, W_V, W_OG, W_LR, W_GA, W_GB = 0, 1024, 2048, 2560, 3072, 4096, 5120, 5136, 6160

ADA_AFTER = {("ya", 0): (4, 5), ("ga", 1): (6, 7), ("ya", 1): (8, 9), ("out", 0): (10, 11)}
PIECES = 4
PK = KT // PIECES
SPLITS = 5


def plan():
    jobs = [("vectors", "dve")]
    jobs += [(("ada", i), "dve") for i in range(4)]
    jobs += [(("uT", t, g), "dve") for t in range(TT) for g in range(2)]
    jobs += [("lr", "act")]
    jobs += [(("gate", t), "dve") for t in range(TT)]
    jobs += [(("v", n, t), "act") for n in range(2) for t in range(TT)]
    jobs += [(("rem", t), "act") for t in range(TT)]
    jobs += [("tot", "act")]
    jobs += [(("k", t), "dve") for t in range(TT)]
    jobs += [(("q", h), "act") for h in range(HEADS)]
    for c in range(NCHUNK + 1):
        if c < NCHUNK:
            jobs += [(("kv", c, g), "dve") for g in range(2)]
        if c >= 1:
            jobs += [(("o", c - 1), "act")]
    for n in range(2):
        jobs += [(("rx", j), "dve") for j in range(4 * n, 4 * n + 4)]
        if n == 0:
            jobs += [(("ss", h), "act") for h in range(HEADS)]
        jobs += [((g, j), "act") for j in range(4 * n, 4 * n + 4) for g in ("ra", "ri")]
    jobs += [(("rg", j), "act") for j in range(KT)]
    jobs += [(("og", j), "act") for j in range(KT)]
    for gate, y in (("gb", "yb"), ("ga", "ya")):
        for n in range(2):
            jobs += [((gate, j), "act") for j in range(4 * n, 4 * n + 4)]
            jobs += [(("ada", i), "dve") for i in ADA_AFTER.get((gate, n), ())]
            jobs += [((y, j), "dve") for j in range(4 * n, 4 * n + 4)]
            jobs += [(("ada", i), "dve") for i in ADA_AFTER.get((y, n), ())]
    for n in range(2):
        jobs += [(("out", n, t), "dve") for t in range(TT)]
        jobs += [(("ada", i), "dve") for i in ADA_AFTER.get(("out", n), ())]
    jobs += [(("u2T", t, g), "act") for t in range(TT) for g in range(2)]
    jobs += [(("router", t), "act") for t in range(TT)]
    jobs += [(("sgu", t), "dve") for t in range(TT)]
    jobs += [("count", "dve"), ("pos", "dve"), ("bstart_col", "dve"), ("bstart_row", "dve"), ("table", "dve")]
    jobs += [(("shT", t), "act") for t in range(TT)]
    jobs += [(("sdown", n, t), "act") for n in range(2) for t in range(TT)]
    return jobs


def layer_program(nc, x, c, ada_w, ada_b, norm1_g, w_in, conv_w, conv_b, rg_wa, rg_ba, rg_wx, rg_bx,
                  rg_lambda, gla_w_up, gla_b_up, gla_norm_g, w_branch_a, w_branch_b, w_out, norm2_g,
                  router_w, router_b, exp_w_gu, exp_w_down, shared_w_gu, shared_w_down, final_g, out):
    jobs = plan()
    J = {name: n for n, (name, _) in enumerate(jobs)}
    emptied_by = [engine for _, engine in jobs]
    emptied_n = [emptied_by[:n + 1].count(emptied_by[n]) for n in range(len(jobs))]

    with ExitStack() as ctx:
        def sb(name, shape, dt=F32, where=ctx):
            return where.enter_context(nc.sbuf_tensor(name, shape, dt))

        def sem(name):
            return ctx.enter_context(nc.semaphore(name))

        psum = ctx.enter_context(nc.psum_tensor("psum", [P, BANKS, NC], F32))

        u2_dram = nc.dram_tensor("u2_rows", (T, D), F32, kind="Internal").ap()
        sum_dram = nc.dram_tensor("expert_sum", (T + P, D), F32, kind="Internal").ap()

        x_tok = sb("x_tok", [P, TT, D])
        ident = sb("ident", [P, P])
        ones = sb("ones", [P, P])
        tri = sb("tri", [P, P], BF16)
        ones_b = sb("ones_b", [P, P], BF16)
        iota_row = sb("iota_row", [P, P])
        block_start = sb("block_start", [P, TABLE])
        eps = sb("eps", [P, 1])
        step_word = sb("step_word", [1, 1])
        dummy_row = sb("dummy_row", [P, 1])
        stat = sb("stat", [P, 8])
        rstd = sb("rstd", [P, 8])
        mods = sb("mods", [P, 8, NC])
        g2_row = mods[:, 6:8, :].rearrange("p a b -> p (a b)")
        row_a = sb("row_a", [P, D])
        tmp_tok = sb("tmp_tok", [P, 2, D])
        ring_place = ExitStack()
        ring = sb("ring", [P, 2, KT, NC], F32, ring_place)
        ring_place.close()
        gu_hi = sb("gu_hi", [P, 2, KT, 2 * DE], F32R)

        mix = ExitStack()
        uT_hi = sb("uT_hi", [P, KT, T], F32R, mix)
        uT_lo = sb("uT_lo", [P, KT, T], F32R, mix)
        w_hi = sb("w_hi", [P, SPLITS, PK, NC], F32R, mix)
        w_lo = sb("w_lo", [P, SPLITS, PK, NC], F32R, mix)
        raw_part = ExitStack()
        oT = sb("oT", [P, KT, T], F32, raw_part)
        gate_w = sb("gate_w", [P, 2, RNN_BLOCKS, P], F32, raw_part)
        raw_part.close()
        o_hi = sb("o_hi", [P, KT, T], F32R, mix)
        o_lo = sb("o_lo", [P, KT, T], F32R, mix)
        hgT = mods[:]
        x_first = mods[:, :, :].rearrange("p (t a) n -> p t (a n)", a=2)
        v_tok = ring[:, 1].rearrange("p (t a) n -> p t (a n)", a=2)
        mT = ring[:, 1]
        er = x_tok[:, 0:2].rearrange("p t (a n) -> p (t a) n", a=2)
        qT = x_tok[:, 2:4].rearrange("p t (a n) -> p (t a) n", a=2)
        tau, xr = er, qT
        tmpT = sb("tmpT", [P, 4, T], F32, mix)
        la = sb("la", [P, TT, NC], F32, mix)
        sh1sc1 = la
        wlr = sb("wlr", [P, KT, RANK], F32, mix)
        wlr_hi = sb("wlr_hi", [P, KT, RANK], F32R, mix)
        wlr_lo = sb("wlr_lo", [P, KT, RANK], F32R, mix)
        lrT = oT[0:32, 1, :]
        wup = oT[0:32, 2, :]
        t1, t2 = tmp_tok[:, 1, 0:T], tmp_tok[:, 1, T:2 * T]
        vec_rows = oT[0:72, 0, 0:P]
        vec = sb("vec", [P, 72], F32, mix)
        sp4 = sb("sp4", [P, 16], F32, mix)
        c_col = sb("c_col", [P, KT], F32, mix)
        decay = sb("decay", [P, HEADS, NCHUNK], F32, mix)
        later = sb("later", [P, P], F32, mix)
        in_chunk = sb("in_chunk", [P, 2], F32, mix)
        state = tmp_tok[:, :, :].rearrange("p s (h v) -> p s h v", h=HEADS)
        CW, CB, BA, BX, LAM, GN = 0, 32, 40, 48, 56, 64
        mix.close()

        moe = ExitStack()
        gu_lo = sb("gu_lo", [P, 2, KT, 2 * DE], F32R, moe)
        gu_raw = sb("gu_raw", [P, KT, 2 * DE], F32, moe)
        w_dn = sb("w_dn", [P, UNROLL, 2, D], F32, moe)
        rows_place = ExitStack()
        u2T = sb("u2T", [P, KT, T], F32, rows_place)
        rows_place.close()
        xT_hi = sb("xT_hi", [P, KT, P], F32R, moe)
        xT_lo = sb("xT_lo", [P, KT, P], F32R, moe)
        over_rest = sb("over_rest", [P, KT, P * 2], F32, moe)
        xg = sb("xg", [P, UNROLL, D], F32, moe)
        xT = sb("xT", [P, KT, P], F32, moe)
        y_rows = sb("y_rows", [P, D], F32, moe)
        router = sb("router", [P, KT, E], F32, moe)
        bias_row = sb("bias_row", [P, E], F32, moe)
        scores = sb("scores", [P, TT, E], F32, moe)
        sel = sb("sel", [P, TT, E], F32, moe)
        slot = sb("slot", [P, TT, E], F32, moe)
        mask = sb("mask", [P, TT, E], F32, moe)
        mask_b = sb("mask_b", [P, TT, E], BF16, moe)
        top8 = sb("top8", [P, TT, TOP_K], F32, moe)
        w3 = sb("w3", [P, TT, E, 3], BF16, moe)
        w_left = sb("w_left", [P, TT, E], F32, moe)
        n_col = sb("n_col", [P, 8], F32, moe)
        nb_rep = sb("nb_rep", [P, P], BF16, moe)
        over = sb("over", [P, TABLE], BF16, moe)
        expert_of = mods[0:1, 2, 0:TABLE].bitcast(U32)
        live_of = mods[0:1, 3, 0:TABLE].bitcast(U32)
        pick = scores[:, 0:2].bitcast(BF16).rearrange("p a (b n) -> p (a b) n", b=2)
        pick_cols = sb("pick_cols", [P, TT, 5], BF16, moe)
        tok_cols = sb("tok_cols", [P, TT, 2], F32, moe)
        got = sb("got", [P, 8], F32, moe)
        row_idx = sb("row_idx", [P, UNROLL, 1], U32, moe)
        order_of = mods[0:1, 4, 0:TABLE].bitcast(U32)
        fresh_of = mods[0:1, 5, 0:TABLE].bitcast(U32)
        add_idx = sb("add_idx", [P, UNROLL, 1], U32, moe)
        live_count = sb("live_count", [1, 1], U32, moe)
        row_w = sb("row_w", [P, UNROLL], F32, moe)
        gate_h = sel[:, 0:2].rearrange("p a n -> p (a n)")
        h_tok = sel[:, 2:4].rearrange("p a n -> p (a n)")
        hT = mask[:, 0:2]
        live_row = xT[0:1, 0:2].rearrange("p a n -> p (a n)")[:, 0:TABLE]
        expert_row = xT[0:1, 2:4].rearrange("p a n -> p (a n)")
        fresh_row = xT[0:1, 4:6].rearrange("p a n -> p (a n)")
        sgate = xT[:, 0:2].rearrange("p a n -> p (a n)")
        sum_tok = u2T[:, :, :].rearrange("p (t a) n -> p t (a n)", a=2)
        moe.close()

        job_done = sem("job_done")
        act_emptied = sem("act_emptied")
        dve_emptied = sem("dve_emptied")
        act_own = sem("act_own")
        dve_own = sem("dve_own")
        pool_own = sem("pool_own")
        consts_ready = sem("consts_ready")
        x_in = sem("x_in")
        c_in = sem("c_in")
        small_in = sem("small_in")
        rows_in = sem("rows_in")
        piece_in = [sem(f"piece_in{p}") for p in range(PIECES)]
        pieces_done = sem("pieces_done")
        hi_ready = sem("hi_ready")
        split_used = sem("split_used")
        shared_in = [sem(f"shared_in{s}") for s in range(2)]
        gates_in = sem("gates_in")
        c_ready = sem("c_ready")
        u_hi = sem("u_hi")
        lr_split = sem("lr_split")
        o_raw, o_hi_ready, o_split = sem("o_raw"), sem("o_hi_ready"), sem("o_split")
        hg_hi, hg_split = sem("hg_hi"), sem("hg_split")
        m_hi, m_split = sem("m_hi"), sem("m_split")
        mods_in = sem("mods_in")
        sums1, sums2, sums3 = [sem(f"sums{i}") for i in (1, 2, 3)]
        roots1, roots2, roots3 = [sem(f"roots{i}") for i in (1, 2, 3)]
        u_ready = sem("u_ready")
        log_ready = sem("log_ready")
        la_ready = sem("la_ready")
        sq_ready = sem("sq_ready")
        og_used = sem("og_used")
        sp_ready = sem("sp_ready")
        ri_ready = sem("ri_ready")
        sqrt_ready = sem("sqrt_ready")
        scan_done = sem("scan_done")
        gated = sem("gated")
        m_ready = sem("m_ready")
        h_res = sem("h_res")
        n2_in = sem("n2_in")
        u2_ready = sem("u2_ready")
        u2_out = [sem(f"u2_out{s}") for s in range(2)]
        fg_in = sem("fg_in")
        router_in = sem("router_in")
        score_ready = sem("score_ready")
        mask_ready = sem("mask_ready")
        nb_ready = sem("nb_ready")
        over_ready = sem("over_ready")
        tables_ready = sem("tables_ready")
        sgate_ready = sem("sgate_ready")
        sh_ready = sem("sh_ready")
        xg_zero = sem("xg_zero")
        w_loaded = [sem(f"w_loaded{s}") for s in range(UNROLL)]
        pick_ready = sem("pick_ready")
        idx_psum = sem("idx_psum")
        idx_ready = sem("idx_ready")
        gathered = [sem(f"gathered{s}") for s in range(UNROLL)]
        xT_psum = sem("xT_psum")
        xT_ready = sem("xT_ready")
        xT_hi_ready = sem("xT_hi_ready")
        gu_in = [sem(f"gu_in{p}") for p in range(PIECES)]
        gu_hi_ready = sem("gu_hi_ready")
        gu_split = sem("gu_split")
        gu_done = sem("gu_done")
        silu_done = sem("silu_done")
        h_ready = sem("h_ready")
        hT_psum = sem("hT_psum")
        hT_ready = sem("hT_ready")
        y_psum = sem("y_psum")
        y_ready = sem("y_ready")
        scattered = sem("scattered")
        experts_done = sem("experts_done")
        found = sem("found")
        add_ready = sem("add_ready")
        step_done = sem("step_done")
        sum_started = sem("sum_started")
        h2_res = sem("h2_res")
        sum_in = sem("sum_in")
        out_ready = sem("out_ready")
        stored = sem("stored")

        def bank(name):
            return psum[:, J[name] % BANKS, :]

        def wait_job(eng, name):
            eng.wait_ge(job_done, J[name] + 1)

        def wait_emptied(eng, name):
            n = J[name]
            eng.wait_ge(act_emptied if emptied_by[n] == "act" else dve_emptied, emptied_n[n])

        class Own:
            def __init__(self, eng, s):
                self.eng, self.s, self.n = eng, s, 0

            def __call__(self, ins):
                self.n += 1
                ins.then_inc(self.s, 1)

            def settle(self):
                self.eng.wait_ge(self.s, self.n)

        wl = w_in[0]
        k_major = lambda w: w.rearrange("(k p) n -> p k n", p=P)
        ada = lambda i: (("ada", i), k_major(ada_w[0])[:, :, i * NC:(i + 1) * NC])
        of_w_in = lambda name, col, n: ((name, n), k_major(wl)[:, :, col + n * NC:col + (n + 1) * NC])
        chunks = [ada(i) for i in range(4)]
        chunks += [of_w_in(name, col, n) for name, col, parts in (("v", W_V, 2), ("k", W_K, 1), ("q", W_Q, 1), ("rx", W_RX, 2), ("rg", W_RG, 2), ("og", W_OG, 2))
                   for n in range(parts)]
        for gate, y, col, w in (("gb", "yb", W_GB, w_branch_b), ("ga", "ya", W_GA, w_branch_a)):
            for n in range(2):
                chunks += [of_w_in(gate, col, n)] + [ada(i) for i in ADA_AFTER.get((gate, n), ())]
                chunks += [((y, n), k_major(w[0])[:, :, n * NC:(n + 1) * NC])] + [ada(i) for i in ADA_AFTER.get((y, n), ())]
        for n in range(2):
            chunks += [(("out", n), k_major(w_out[0])[:, :, n * NC:(n + 1) * NC])] + [ada(i) for i in ADA_AFTER.get(("out", n), ())]
        C = {name: n for n, (name, _) in enumerate(chunks)}
        split_names = [name for name, _ in chunks if name[0] != "ada"]
        S = {name: n for n, name in enumerate(split_names)}

        def last_job(name):
            kind, n = name
            return (kind, n, TT - 1) if kind in ("v", "out") else (kind, 4 * n + 3)

        def raw(p):
            return ring[:, 0, PK * p:PK * p + PK]

        def place_of(name, p):
            return (PIECES * S[name] + p) % SPLITS

        def split_hi(act, name):
            for p in range(PIECES):
                act.wait_ge(piece_in[p], 16 * (C[name] + 1))
                before = PIECES * S[name] + p - SPLITS
                if before >= 0:
                    m, q = divmod(before, PIECES)
                    if q < PIECES - 1:
                        act.wait_ge(split_used, (PIECES - 1) * m + q + 1)
                    else:
                        wait_job(act, last_job(split_names[m]))
                act.activation(w_hi[:, place_of(name, p)], raw(p), ACT.Copy).then_inc(hi_ready, 1)

        def split_lo(dve, name):
            for p in range(PIECES):
                at = place_of(name, p)
                dve.wait_ge(hi_ready, PIECES * S[name] + p + 1)
                dve.tensor_tensor(w_lo[:, at], raw(p), w_hi[:, at].bitcast(F32), ALU.subtract).then_inc(pieces_done, 1)

        sgu_w = ring[:, 0]
        sdown_w = ring[:, 1, 0:4].rearrange("p (j a) n -> p j (a n)", j=2)
        sh_tok = ring[:, 1, 4:6].rearrange("p a (t n) -> p (a t) n", n=DE)
        shT = ring[:, 1, 6:8]

        expert_gu = exp_w_gu[0].rearrange("e (p k) f -> e p k f", k=KT)
        expert_dn = exp_w_down[0].rearrange("e (j p) n -> e p j n", p=P)
        x_rows = x[0].rearrange("(t p) d -> p t d", p=P)
        SMALL = 5
        GU, HT, IDX, Y0 = 2, 3, 4, 5
        moe_bank = lambda n: psum[:, n, :]

        def live_blocks(eng, ask=True):
            with eng.Fori(0, SPANS) as span:
                live_span = eng.value_load(live_of[0:1, bass.ds(span * (SPAN * UNROLL), 1)], min_val=0, max_val=1)
                with eng.If(live_span > 0):
                    with eng.Fori(0, SPAN) as group:
                        i = span * SPAN + group
                        for s in range(UNROLL):
                            b = i * UNROLL + s
                            if not ask:
                                yield i, s, b
                                continue
                            live = eng.value_load(live_of[0:1, bass.ds(b, 1)], min_val=0, max_val=1)
                            with eng.If(live > 0):
                                yield i, s, b
                    eng.nop()

        block = ctx.enter_context(nc.Block())

        @block.sync
        def _(sp):
            for n, (name, src) in enumerate(chunks):
                for p in range(PIECES):
                    if n:
                        sp.wait_ge(pieces_done, PIECES * (n - 1) + p + 1)
                    sp.dma_start(raw(p), src[:, PK * p:PK * p + PK]).then_inc(piece_in[p], 16)
            sp.wait_ge(pieces_done, PIECES * len(chunks))
            sp.dma_start(sgu_w, k_major(shared_w_gu[0])).then_inc(shared_in[0], 16)
            sp.wait_ge(m_split, KT)
            sp.dma_start(sdown_w, shared_w_down[0].rearrange("(j p) n -> p j n", p=P)).then_inc(shared_in[1], 16)
            wait_job(sp, ("out", 1, TT - 1))
            wait_emptied(sp, ("out", 1, TT - 1))
            sp.wait_ge(tables_ready, 1)

            def load_down(b, s, done=None):
                live = sp.value_load(live_of[0:1, bass.ds(b, 1)], min_val=0, max_val=1)
                with sp.If(live > 0):
                    e = sp.value_load(expert_of[0:1, bass.ds(b, 1)], min_val=0, max_val=E - 1)
                    fresh = sp.value_load(fresh_of[0:1, bass.ds(b, 1)], min_val=0, max_val=1)
                    order = sp.value_load(order_of[0:1, bass.ds(b, 1)], min_val=0, max_val=E)
                    place = order % UNROLL
                    if done is not None:
                        sp.wait_ge(y_psum, done)
                    sp.dma_start(w_dn[:, bass.ds(place, 1)].rearrange("p o j n -> p (o j) n"), expert_dn[bass.ds(e, 1)].rearrange("o p j n -> p (o j) n"),
                                 cond=fresh > 0, bounds_check="skip_entire_dma").then_inc(w_loaded[s], 16)

            def load_gu(b, first=False):
                fresh = sp.value_load(fresh_of[0:1, bass.ds(b, 1)], min_val=0, max_val=1)
                with sp.If(fresh > 0):
                    e = sp.value_load(expert_of[0:1, bass.ds(b, 1)], min_val=0, max_val=E - 1)
                    order = sp.value_load(order_of[0:1, bass.ds(b, 1)], min_val=0, max_val=E)
                    for p in range(PIECES):
                        if not first:
                            sp.wait_ge(gu_split, order * PIECES + p + 1)
                        sp.dma_start(gu_raw[:, PK * p:PK * p + PK], expert_gu[bass.ds(e, 1), :, PK * p:PK * p + PK].rearrange("o p k f -> p (o k) f")).then_inc(gu_in[p], 16)

            load_gu(0, first=True)
            load_down(0, 0)
            load_gu(1)
            load_down(1, 1)
            load_gu(2)
            load_down(2, 2)
            for i, s, b in live_blocks(sp, ask=False):
                load_gu(b + UNROLL)
                load_down(b + UNROLL, s, 2 * b + 4)
            sp.wait_ge(experts_done, 1)
            sp.dma_start(sum_tok, sum_dram[0:T].rearrange("(t p) d -> p t d", p=P)).then_inc(sum_in, 16)
            for t in range(TT):
                sp.wait_ge(out_ready, t + 1)
                sp.dma_start(out[0].rearrange("(t p) d -> p t d", p=P)[:, t], x_tok[:, t]).then_inc(stored, 16)
            sp.wait_ge(stored, 16 * TT)

        @block.gpsimd
        def _(pool):
            count = Own(pool, pool_own)

            def own(ins):
                count(ins)
                count.settle()

            own(pool.memset(ident[:], 0.0))
            own(pool.memset(ones[:], 1.0))
            own(pool.memset(ones_b[:], 1.0))
            own(pool.memset(later[:], 1.0))
            own(pool.memset(tri[:], 1.0))
            own(pool.memset(in_chunk[:], 0.0))
            own(pool.memset(eps[:], EPS))
            own(pool.memset(lrT, 1.0))
            own(pool.affine_select(ident[:], ident[:], [[-1, P]], ALU.not_equal, 1.0, base=0, channel_multiplier=1))
            own(pool.affine_select(later[:], later[:], [[-1, P]], ALU.is_gt, 0.0, base=0, channel_multiplier=1))
            own(pool.affine_select(tri[:], tri[:], [[1, P]], ALU.is_gt, 0.0, base=0, channel_multiplier=-1))
            own(pool.memset(in_chunk[0:CHUNK, 0:1], 1.0))
            own(pool.memset(in_chunk[CHUNK:P, 1:2], 1.0))
            own(pool.iota(iota_row[:], [[1, P]], base=0, channel_multiplier=0, allow_small_or_imprecise_dtypes=True))
            own(pool.iota(block_start[:], [[P, TABLE]], base=0, channel_multiplier=0, allow_small_or_imprecise_dtypes=True))
            own(pool.iota(dummy_row[:], [[0, 1]], base=T + 1, channel_multiplier=1, allow_small_or_imprecise_dtypes=True))
            own(pool.memset(later[CHUNK:P, 0:CHUNK], 0.0))
            pool.nop().then_inc(consts_ready, 1)
            wait_job(pool, ("out", 1, TT - 1))
            pool.memset(xg[:], 0.0).then_inc(xg_zero, 1)
            own(pool.iota(tok_cols[:, :, 0:1], [[0, TT], [0, 1]], base=1, channel_multiplier=1, allow_small_or_imprecise_dtypes=True))
            own(pool.iota(tok_cols[:, :, 1:2], [[P, TT], [0, 1]], base=0, channel_multiplier=0, allow_small_or_imprecise_dtypes=True))
            pool.nop().then_inc(xg_zero, 1)
            for t in range(2):
                pool.wait_ge(u2_out[t % 2], 32)
            pool.wait_ge(sum_started, 16)
            pool.wait_ge(xg_zero, 1)
            pool.dma_start(sum_dram[T:T + P], xg[:, 0]).then_inc(scattered, 16)
            pool.wait_ge(scattered, 16)
            pool.wait_ge(tables_ready, 1)

            def step(n):
                if not isinstance(n, int) or n > 0:
                    pool.wait_ge(step_done, n)
                pool.tensor_tensor(step_word[:], ones[0:1, 0:1], ones[0:1, 0:1], ALU.mult).then_inc(step_done, 1)

            def gather(b, s, n):
                pool.wait_ge(idx_ready, b + 1)
                step(n)
                pool.indirect_dma_start(xg[:, s], None, u2_dram, bass.IndirectOffsetOnAxis(row_idx[:, s], 0),
                                        bounds_check=T - 1, oob_is_err=False).then_inc(gathered[s], 16)

            gather(0, 0, 0)
            gather(1, 1, 1)
            for i, s, b in live_blocks(pool):
                pool.wait_ge(xT_psum, 2 * b + 2)
                gather(b + 2, (s + 2) % UNROLL, 2 * b + 2)
                pool.wait_ge(scattered, 16 * b + 16)
                pool.wait_ge(y_ready, 2 * b + 4)
                pool.wait_ge(add_ready, b + 1)
                step(2 * b + 3)
                pool.indirect_dma_start(sum_dram, bass.IndirectOffsetOnAxis(add_idx[:, s], 0), y_rows[:], None,
                                        compute_op=ALU.add, bounds_check=T + P - 1, oob_is_err=True).then_inc(scattered, 16)
            live_n = pool.value_load(live_count[0:1, 0:1], min_val=1, max_val=MOE_BLOCKS)
            pool.wait_ge(scattered, 16 * live_n + 16)
            pool.wait_ge(step_done, 2 * live_n + 2)
            pool.tensor_tensor(step_word[:], ones[0:1, 0:1], ones[0:1, 0:1], ALU.mult).then_inc(experts_done, 1)

        @block.scalar
        def _(act):
            own = Own(act, act_own)
            act.dma_start(c_col[:], c.rearrange("o (k p) -> p (o k)", p=P), allow_slow_non_contiguous=True).then_inc(c_in, 16)
            act.dma_start(x_first, x_rows).then_inc(x_in, 16)
            act.dma_start(vec_rows[CW:CW + 32, :], conv_w[0].rearrange("j (k p) -> (j k) p", p=P)).then_inc(rows_in, 16)
            for at, v in ((CB, conv_b), (BA, rg_ba), (BX, rg_bx), (LAM, rg_lambda)):
                act.dma_start(vec_rows[at:at + 8, :], v.rearrange("o (k p) -> (o k) p", p=P)).then_inc(rows_in, 16)
            act.dma_start(vec_rows[GN:GN + 8, :], gla_norm_g[0].rearrange("h (k p) -> (h k) p", p=P)).then_inc(rows_in, 16)
            act.dma_start(row_a[:], norm1_g.broadcast_to([P, D])).then_inc(small_in, 16)
            act.dma_start(sh1sc1[:].rearrange("p a n -> p (a n)"), ada_b[:, 0:4 * NC].broadcast_to([P, 4 * NC])).then_inc(small_in, 16)
            act.dma_start(wlr[:], k_major(wl)[:, :, W_LR:W_LR + RANK]).then_inc(small_in, 16)
            act.dma_start(wup[0:RANK, :], gla_w_up[0]).then_inc(small_in, 16)
            act.dma_start(wup[RANK:RANK + 1, :], gla_b_up).then_inc(small_in, 16)
            act.dma_start(gate_w[:, 0], rg_wa[0].rearrange("j p n -> p j n")).then_inc(gates_in, 16)
            act.dma_start(gate_w[:, 1], rg_wx[0].rearrange("j p n -> p j n")).then_inc(gates_in, 16)
            act.wait_ge(c_in, 16)
            act.activation(c_col[:], c_col[:], ACT.Silu).then_inc(c_ready, 1)
            act.wait_ge(x_in, 16)
            for t in range(TT):
                if t:
                    act.wait_ge(sums1, t)
                act.activation(tmp_tok[:, 0], x_first[:, t], ACT.Square, accum_out=stat[:, t:t + 1]).then_inc(sums1, 1)
            act.wait_ge(sums1, TT)
            act.wait_ge(consts_ready, 1)
            act.activation(rstd[:, 0:TT], stat[:, 0:TT], ACT.Sqrt, bias=eps[:], scale=1.0 / D).then_inc(roots1, 1)
            act.wait_ge(small_in, 16 * SMALL)
            act.activation(wlr_hi[:], wlr[:], ACT.Copy).then_inc(lr_split, 1)
            for t in range(TT):
                for g in range(2):
                    wait_job(act, ("uT", t, g))
                    act.activation(uT_hi[:, 4 * g:4 * g + 4, t * P:(t + 1) * P], bank(("uT", t, g)).rearrange("p (k n) -> p k n", k=4), ACT.Copy).then_inc(u_hi, 1)
            split_hi(act, ("v", 0))
            wait_job(act, "lr")
            act.activation(lrT[0:RANK, :], bank("lr")[0:RANK, :], ACT.Copy).then_inc(act_emptied, 1)
            for t in range(TT):
                wait_emptied(act, ("gate", t))
                own(act.activation(er[:, t], la[:, t], ACT.Abs))
                own.settle()
                own(act.activation(er[:, t], er[:, t], ACT.Exp, scale=-1.0))
                own.settle()
                act.activation(er[:, t], er[:, t], ACT.Ln, bias=1.0).then_inc(log_ready, 1)
            wait_emptied(act, "vectors")
            own(act.activation(sp4[:, 0:8], vec[:, LAM:LAM + 8], ACT.Abs))
            own.settle()
            own(act.activation(sp4[:, 0:8], sp4[:, 0:8], ACT.Exp, scale=-1.0))
            own.settle()
            act.activation(sp4[:, 0:8], sp4[:, 0:8], ACT.Ln, bias=1.0).then_inc(sp_ready, 1)
            for n in range(2):
                for t in range(TT):
                    if t == TT - 1:
                        split_hi(act, (("v", 1), ("k", 0))[n])
                    wait_job(act, ("v", n, t))
                    act.activation(v_tok[:, t, n * NC:(n + 1) * NC], bank(("v", n, t)), ACT.Copy).then_inc(act_emptied, 1)
            for t in range(TT):
                act.wait_ge(la_ready, t + 1)
                wait_job(act, ("rem", t))
                act.activation(er[:, t], bank(("rem", t)), ACT.Exp, scale=1.0 / 16).then_inc(act_emptied, 1)
            wait_job(act, "tot")
            act.activation(decay[:], bank("tot")[:, 0:HEADS * NCHUNK].rearrange("p (h n) -> p h n", h=HEADS), ACT.Exp, scale=1.0 / 16).then_inc(act_emptied, 1)
            split_hi(act, ("q", 0))
            for h in range(HEADS):
                if h == HEADS - 1:
                    split_hi(act, ("rx", 0))
                wait_job(act, ("q", h))
                act.activation(qT[:, h], bank(("q", h)), ACT.Copy, scale=DK ** -0.5).then_inc(act_emptied, 1)
            for n in range(NCHUNK):
                wait_job(act, ("o", n))
                act.activation(oT[:, :, n * CHUNK:(n + 1) * CHUNK], bank(("o", n)).rearrange("p (k n) -> p k n", k=KT), ACT.Copy).then_inc(act_emptied, 1)
            wait_emptied(act, ("o", NCHUNK - 1))
            for h in range(HEADS):
                if h >= 2:
                    wait_job(act, ("ss", h - 2))
                act.activation(tmpT[:, 2 * (h % 2):2 * (h % 2) + 2], oT[:, 2 * h:2 * h + 2], ACT.Square).then_inc(sq_ready, 1)
            for h in range(HEADS):
                wait_job(act, ("ss", h))
                act.activation(la[:, h], bank(("ss", h)), ACT.Sqrt, bias=eps[:], scale=1.0 / DV).then_inc(act_emptied, 1)
            for n in range(2):
                split_hi(act, (("rx", 1), ("rg", 0))[n])
                for q in range(4):
                    j = 4 * n + q
                    wait_job(act, ("ra", j))
                    if n == 0:
                        act.wait_ge(sp_ready, 2)
                    else:
                        act.wait_ge(scan_done, q + 1)
                    own(act.activation(tau[:, q], bank(("ra", j)), ACT.Sigmoid, bias=vec[:, BA + j:BA + j + 1]))
                    own.settle()
                    act.activation(tau[:, q], tau[:, q], ACT.Tanh, scale=sp4[:, 8 + j:9 + j]).then_inc(act_emptied, 1)
                    wait_job(act, ("ri", j))
                    act.activation(tmpT[:, q], bank(("ri", j)), ACT.Sigmoid, bias=vec[:, BX + j:BX + j + 1]).then_inc(act_emptied, 1)
                for q in range(4):
                    j = 4 * n + q
                    act.wait_ge(ri_ready, j + 1)
                    wait_emptied(act, ("ra", j))
                    act.activation(tmpT[:, q], tau[:, q], ACT.Sqrt).then_inc(sqrt_ready, 1)
            for j in range(KT):
                if j % 4 == 3:
                    split_hi(act, (("rg", 1), ("og", 0))[j // 4])
                wait_job(act, ("rg", j))
                if j < 4:
                    act.wait_ge(scan_done, j + 5)
                else:
                    act.wait_ge(gated, j - 3)
                act.activation(tmpT[:, j % 4], bank(("rg", j)), ACT.Gelu_apprx_tanh).then_inc(act_emptied, 1)
            act.wait_ge(scan_done, KT)
            act.dma_start(x_tok[:], x_rows).then_inc(x_in, 16)

            def head_hi(j):
                act.wait_ge(o_raw, j + 1)
                act.activation(o_hi[:, j], (t1, t2)[j % 2], ACT.Copy).then_inc(o_hi_ready, 1)

            for j in range(KT):
                if j % 4 == 3:
                    split_hi(act, (("og", 1), ("gb", 0))[j // 4])
                wait_job(act, ("og", j))
                if j >= 4:
                    act.wait_ge(o_raw, j - 3)
                else:
                    act.wait_ge(gated, j + 5)
                act.activation(tmpT[:, j % 4], bank(("og", j)), ACT.Silu).then_inc(act_emptied, 1)
                if j:
                    head_hi(j - 1)
            head_hi(KT - 1)
            for gate, y in (("gb", "yb"), ("ga", "ya")):
                for j in range(KT):
                    if j % 4 == 3:
                        split_hi(act, (y, j // 4))
                    wait_job(act, (gate, j))
                    if gate == "gb" and j < 4:
                        act.wait_ge(o_raw, j + 5)
                    elif j >= 4:
                        wait_emptied(act, (y, j - 4))
                    else:
                        wait_emptied(act, ("yb", j + 4))
                    act.activation(tmpT[:, j % 4], bank((gate, j)), ACT.Sigmoid).then_inc(act_emptied, 1)
                    if j == 3:
                        if gate == "ga":
                            act.wait_ge(hg_split, KT)
                            act.dma_start(mods[:].rearrange("p a n -> p (a n)"), ada_b[:, 4 * NC:12 * NC].broadcast_to([P, 8 * NC])).then_inc(mods_in, 16)
                        split_hi(act, (gate, 1))
                if gate == "gb":
                    split_hi(act, ("ga", 0))
                    wait_job(act, ("yb", KT - 1))
                    for j in range(KT):
                        act.wait_ge(gated, j + 1)
                        act.activation(o_hi[:, j], hgT[:, j], ACT.Copy).then_inc(hg_hi, 1)
            wait_job(act, ("ga", KT - 1))
            for j in range(KT):
                if j == 4:
                    split_hi(act, ("out", 0))
                act.wait_ge(m_ready, j + 1)
                act.activation(uT_hi[:, j], mT[:, j], ACT.Copy).then_inc(m_hi, 1)
            split_hi(act, ("out", 1))
            act.dma_start(row_a[:], norm2_g.broadcast_to([P, D])).then_inc(n2_in, 16)
            act.wait_ge(h_res, TT)
            wait_emptied(act, ("ada", 11))
            act.dma_start(router[:], k_major(router_w[0])).then_inc(router_in, 16)
            act.dma_start(bias_row[:], router_b.broadcast_to([P, E])).then_inc(router_in, 16)
            for t in range(TT):
                act.wait_ge(h_res, TT + t + 1)
                act.activation(xT[:].rearrange("p k n -> p (k n)"), x_tok[:, t], ACT.Square, accum_out=stat[:, 4 + t:5 + t]).then_inc(sums2, 1)
                act.wait_ge(sums2, t + 1)
                act.activation(rstd[:, 4 + t:5 + t], stat[:, 4 + t:5 + t], ACT.Sqrt, bias=eps[:], scale=1.0 / D).then_inc(roots2, 1)
            for t in range(TT):
                act.wait_ge(u2_ready, t + 1)
                act.dma_start(u2_dram.rearrange("(t p) d -> p t d", p=P)[:, t], tmp_tok[:, t % 2]).then_inc(u2_out[t % 2], 16)
                for g in range(2):
                    wait_job(act, ("u2T", t, g))
                    act.activation(u2T[:, 4 * g:4 * g + 4, t * P:(t + 1) * P], bank(("u2T", t, g)).rearrange("p (k n) -> p k n", k=4), ACT.Copy).then_inc(act_emptied, 1)
            for t in range(TT):
                wait_job(act, ("router", t))
                act.activation(scores[:, t], bank(("router", t))[:, 0:E], ACT.Sigmoid).then_inc(act_emptied, 1)
            act.dma_start(row_a[:], final_g.rearrange("(o d) -> o d", o=1).broadcast_to([P, D])).then_inc(fg_in, 16)
            for t in range(TT):
                wait_job(act, ("sgu", t))
                if t:
                    wait_emptied(act, ("sgu", t - 1))
                act.activation(sgate, bank(("sgu", t))[:, 0:DE], ACT.Silu).then_inc(sgate_ready, 1)
            for t in range(TT):
                wait_job(act, ("shT", t))
                act.activation(shT[:, :, t * P:(t + 1) * P], bank(("shT", t))[:, 0:2 * P].rearrange("p (j n) -> p j n", j=2), ACT.Copy).then_inc(act_emptied, 1)
            for n in range(2):
                for t in range(TT):
                    wait_job(act, ("sdown", n, t))
                    act.activation(sum_tok[:, t, n * NC:(n + 1) * NC], bank(("sdown", n, t)), ACT.Copy).then_inc(act_emptied, 1)
            wait_emptied(act, ("sdown", 1, TT - 1))
            act.dma_start(sum_dram[0:T].rearrange("(t p) d -> p t d", p=P), sum_tok).then_inc(sum_started, 16)

            def turned_rows(n):
                for g in range(2):
                    act.wait_ge(xT_psum, 2 * n + 1 + g)
                    act.activation(xT_hi[:, 4 * g:4 * g + 4], moe_bank(g).rearrange("p (k n) -> p k n", k=4), ACT.Copy).then_inc(xT_hi_ready, 1)

            def expert_hi(n):
                fresh = act.value_load(fresh_of[0:1, bass.ds(n, 1)], min_val=0, max_val=1)
                with act.If(fresh > 0):
                    order = act.value_load(order_of[0:1, bass.ds(n, 1)], min_val=0, max_val=E)
                    for p in range(PIECES):
                        act.wait_ge(gu_in[p], order * 16 + 16)
                        act.activation(gu_hi[:, bass.ds(order % 2, 1), PK * p:PK * p + PK].rearrange("p o k f -> p (o k) f"),
                                       gu_raw[:, PK * p:PK * p + PK], ACT.Copy).then_inc(gu_hi_ready, 1)

            act.wait_ge(tables_ready, 1)
            act.wait_ge(sum_started, 16)
            expert_hi(0)
            expert_hi(1)
            turned_rows(0)
            act.nop().then_inc(y_ready, 2)
            for i, s, b in live_blocks(act):
                act.wait_ge(gu_done, b + 1)
                act.wait_ge(h_ready, b + 1)
                act.activation(gate_h, moe_bank(GU)[:, 0:DE], ACT.Silu).then_inc(silu_done, 1)
                turned_rows(b + 1)
                expert_hi(b + 2)
                act.wait_ge(idx_ready, b + 1)
                act.wait_ge(scattered, 16 * b + 16)
                for g in range(2):
                    act.wait_ge(y_psum, 2 * b + 3 + g)
                    act.activation(y_rows[:, g * NC:(g + 1) * NC], moe_bank(Y0 + g), ACT.Copy, scale=row_w[:, s:s + 1]).then_inc(y_ready, 1)
            for t in range(TT):
                act.wait_ge(h2_res, t + 1)
                act.activation(xT[:].rearrange("p k n -> p (k n)"), x_tok[:, t], ACT.Square, accum_out=stat[:, t:t + 1]).then_inc(sums3, 1)
                act.wait_ge(sums3, t + 1)
                act.activation(rstd[:, t:t + 1], stat[:, t:t + 1], ACT.Sqrt, bias=eps[:], scale=1.0 / D).then_inc(roots3, 1)

        @block.vector
        def _(dve):
            own = Own(dve, dve_own)
            tt, ts, stt = dve.tensor_tensor, dve.tensor_scalar, dve.scalar_tensor_tensor
            wait_job(dve, "vectors")
            dve.tensor_copy(vec[:], bank("vectors")[:, 0:72]).then_inc(dve_emptied, 1)
            dve.wait_ge(small_in, 16 * SMALL)
            def ada_sum(i, acc):
                c0 = C[("ada", i)]
                if i in (2, 3) or i >= 6:
                    wait_job(dve, ("ada", i - 2))
                for p in range(PIECES):
                    dve.wait_ge(piece_in[p], 16 * (c0 + 1))
                    if p:
                        dve.wait_ge(pieces_done, PIECES * c0 + p)
                        own(stt(acc, raw(p)[:, 0], c_col[:, PK * p:PK * p + 1], acc, ALU.mult, ALU.add))
                    else:
                        own(ts(acc, raw(p)[:, 0], c_col[:, 0:1], None, ALU.mult))
                    own.settle()
                    stt(acc, raw(p)[:, 1], c_col[:, PK * p + 1:PK * p + 2], acc, ALU.mult, ALU.add).then_inc(pieces_done, 1)

            def ada_row(i, row):
                wait_job(dve, ("ada", i))
                tt(row, bank(("ada", i)), row, ALU.add).then_inc(dve_emptied, 1)

            dve.wait_ge(c_ready, 1)
            for i in range(4):
                ada_sum(i, tmpT[:, i % 2])
                if i:
                    ada_row(i - 1, sh1sc1[:, i - 1])
            ada_row(3, sh1sc1[:, 3])
            wait_emptied(dve, ("ada", 3))
            own(stt(row_a[:], sh1sc1[:, 2:4].rearrange("p a n -> p (a n)"), 1.0, row_a[:], ALU.add, ALU.mult))
            dve.wait_ge(roots1, 1)
            own(dve.reciprocal(rstd[:, 0:TT], rstd[:, 0:TT]))
            own.settle()

            def u_lo(t):
                for g in range(2):
                    dve.wait_ge(u_hi, 2 * t + g + 1)
                    at = uT_lo[:, 4 * g:4 * g + 4, t * P:(t + 1) * P]
                    tt(at, bank(("uT", t, g)).rearrange("p (k n) -> p k n", k=4),
                       uT_hi[:, 4 * g:4 * g + 4, t * P:(t + 1) * P].bitcast(F32), ALU.subtract).then_inc(dve_emptied, 1)

            for t in range(TT):
                if t >= 2:
                    wait_job(dve, ("uT", t - 2, 1))
                own(stt(tmp_tok[:, t % 2], x_first[:, t], rstd[:, t:t + 1], row_a[:], ALU.mult, ALU.mult))
                own.settle()
                tt(tmp_tok[:, t % 2], tmp_tok[:, t % 2], sh1sc1[:, 0:2].rearrange("p a n -> p (a n)"), ALU.add).then_inc(u_ready, 1)
                if t == 0:
                    dve.wait_ge(lr_split, 1)
                    tt(wlr_lo[:], wlr[:], wlr_hi[:].bitcast(F32), ALU.subtract).then_inc(lr_split, 1)
                else:
                    u_lo(t - 1)
            u_lo(TT - 1)
            split_lo(dve, ("v", 0))
            dve.wait_ge(u_ready, TT)
            for t in range(TT):
                wait_job(dve, ("gate", t))
                dve.tensor_copy(la[:, t], bank(("gate", t))).then_inc(dve_emptied, 1)
            for t in range(TT):
                dve.wait_ge(log_ready, t + 1)
                stt(la[:, t], la[:, t], 0.0, er[:, t], ALU.min, ALU.subtract).then_inc(la_ready, 1)
            dve.wait_ge(sp_ready, 1)
            own(stt(sp4[:, 0:8], vec[:, LAM:LAM + 8], 0.0, sp4[:, 0:8], ALU.min, ALU.subtract))
            own.settle()
            ts(sp4[:, 8:16], sp4[:, 0:8], -RG_C / 2, None, ALU.mult).then_inc(sp_ready, 1)
            split_lo(dve, ("v", 1))
            split_lo(dve, ("k", 0))
            for t in range(TT):
                if t == TT - 1:
                    split_lo(dve, ("q", 0))
                wait_job(dve, ("k", t))
                wait_emptied(dve, ("rem", t))
                tt(er[:, t], bank(("k", t)), er[:, t], ALU.mult).then_inc(dve_emptied, 1)
            split_lo(dve, ("rx", 0))
            wait_emptied(dve, "tot")
            for n in range(NCHUNK):
                if n >= 2:
                    wait_job(dve, ("o", n - 2))
                if n >= 1:
                    wait_emptied(dve, ("kv", n - 1, 1))
                for g in range(2):
                    wait_job(dve, ("kv", n, g))
                    for h in range(2 * g, 2 * g + 2):
                        kv = bank(("kv", n, g))[:, (h % 2) * DV:(h % 2 + 1) * DV]
                        if n == 0:
                            ins = dve.tensor_copy(state[:, 0, h], kv)
                        else:
                            ins = stt(state[:, n % 2, h], state[:, (n - 1) % 2, h], decay[:, h, n:n + 1], kv, ALU.mult, ALU.add)
                        if h % 2 == 0:
                            own(ins)
                    ins.then_inc(dve_emptied, 1)
            for n in range(2):
                for q in range(4):
                    j = 4 * n + q
                    wait_job(dve, ("rx", j))
                    rx = bank(("rx", j))
                    tap = lambda d: vec[:, CW + 8 * (CONV_W - 1 - d) + j:CW + 8 * (CONV_W - 1 - d) + j + 1]
                    own(ts(xr[:, q], rx, tap(0), vec[:, CB + j:CB + j + 1], ALU.mult, ALU.add))
                    for d in range(1, CONV_W):
                        own.settle()
                        ins = stt(xr[:, q, d:T], rx[:, 0:T - d], tap(d), xr[:, q, d:T], ALU.mult, ALU.add)
                        if d < CONV_W - 1:
                            own(ins)
                    ins.then_inc(dve_emptied, 1)
                split_lo(dve, (("rx", 1), ("rg", 0))[n])
                for q in range(4):
                    j = 4 * n + q
                    wait_emptied(dve, ("ri", j))
                    tt(xr[:, q], xr[:, q], tmpT[:, q], ALU.mult).then_inc(ri_ready, 1)
                dve.wait_ge(ri_ready, 4 * n + 4)
                for q in range(4):
                    j = 4 * n + q
                    dve.wait_ge(sqrt_ready, j + 1)
                    own(ts(t1, tau[:, q], 1.0, None, ALU.add))
                    own.settle()
                    own(dve.reciprocal(t1, t1))
                    own.settle()
                    own(stt(t2, tmpT[:, q], 2.0, t1, ALU.mult, ALU.mult))
                    own(ts(tau[:, q], t1, 2.0, -1.0, ALU.mult, ALU.add))
                    own.settle()
                    own(dve.memset(t2[:, 0:1], 1.0))
                    own.settle()
                    own(tt(xr[:, q], xr[:, q], t2, ALU.mult))
                    own.settle()
                    dve.tensor_tensor_scan(hgT[:, j], tau[:, q], xr[:, q], 0.0, ALU.mult, ALU.add).then_inc(scan_done, 1)
            dve.wait_ge(scan_done, KT)
            split_lo(dve, ("rg", 1))
            for j in range(KT):
                if j == KT - 1:
                    split_lo(dve, ("og", 0))
                wait_emptied(dve, ("rg", j))
                tt(hgT[:, j], hgT[:, j], tmpT[:, j % 4], ALU.mult).then_inc(gated, 1)

            def head_lo(j):
                dve.wait_ge(o_hi_ready, j + 1)
                tt(o_lo[:, j], (t1, t2)[j % 2], o_hi[:, j].bitcast(F32), ALU.subtract).then_inc(o_split, 1)

            for j in range(KT):
                h = j // 2
                if j % 4 == 3:
                    split_lo(dve, (("og", 1), ("gb", 0))[j // 4])
                if j % 2 == 0:
                    wait_emptied(dve, ("ss", h))
                    own(dve.reciprocal(la[:, h], la[:, h]))
                    own.settle()
                own(stt(oT[:, j], oT[:, j], vec[:, GN + j:GN + j + 1], la[:, h], ALU.mult, ALU.mult))
                own.settle()
                wait_emptied(dve, ("og", j))
                if j >= 2:
                    dve.wait_ge(o_split, j - 1)
                tt((t1, t2)[j % 2], oT[:, j], tmpT[:, j % 4], ALU.mult).then_inc(o_raw, 1)
                if j:
                    head_lo(j - 1)
            head_lo(KT - 1)
            dve.wait_ge(o_split, KT)
            split_lo(dve, ("yb", 0))
            for j in range(KT):
                if j % 4 == 3:
                    split_lo(dve, (("gb", 1), ("ga", 0))[j // 4])
                if j == 4:
                    split_lo(dve, ("yb", 1))
                wait_emptied(dve, ("gb", j))
                wait_job(dve, ("yb", j))
                tt(mT[:, j], bank(("yb", j)), tmpT[:, j % 4], ALU.mult).then_inc(dve_emptied, 1)
            for j in range(KT):
                dve.wait_ge(hg_hi, j + 1)
                tt(o_lo[:, j], hgT[:, j], o_hi[:, j].bitcast(F32), ALU.subtract).then_inc(hg_split, 1)
            split_lo(dve, ("ya", 0))

            def merged_lo(j):
                dve.wait_ge(m_hi, j + 1)
                tt(uT_lo[:, j], mT[:, j], uT_hi[:, j].bitcast(F32), ALU.subtract).then_inc(m_split, 1)

            wait_emptied(dve, ("yb", KT - 1))
            for j in range(KT):
                wait_emptied(dve, ("ga", j))
                wait_job(dve, ("ya", j))
                if j:
                    dve.wait_ge(m_ready, j)
                tt(t1, bank(("ya", j)), tmpT[:, j % 4], ALU.mult).then_inc(dve_emptied, 1)
                wait_emptied(dve, ("ya", j))
                tt(mT[:, j], mT[:, j], t1, ALU.add).then_inc(m_ready, 1)
                if j % 4 < 2:
                    i = (4 if j < 4 else 8) + j % 4
                    ada_sum(i, la[:, i % 2])
                if j == 2:
                    split_lo(dve, ("ga", 1))
                if j == 3:
                    dve.wait_ge(mods_in, 16)
                    for i in (4, 5):
                        ada_row(i, mods[:, i - 4])
                    for i in (6, 7):
                        ada_sum(i, la[:, i % 2])
                    split_lo(dve, ("ya", 1))
                    for i in (6, 7):
                        ada_row(i, mods[:, i - 4])
                    for m in range(4):
                        merged_lo(m)
                if j == 6:
                    split_lo(dve, ("out", 0))
                    for m in range(4, 7):
                        merged_lo(m)
            merged_lo(7)
            for i in (8, 9):
                ada_row(i, mods[:, i - 4])
            for n in range(2):
                for t in range(TT):
                    if (n, t) == (0, TT - 1):
                        split_lo(dve, ("out", 1))
                    wait_job(dve, ("out", n, t))
                    if n == 0 and t == 0:
                        dve.wait_ge(m_ready, KT)
                        dve.wait_ge(x_in, 32)
                    if n or t:
                        dve.wait_ge(h_res, TT * n + t)
                    tt(t1, bank(("out", n, t)), mods[:, n], ALU.mult).then_inc(dve_emptied, 1)
                    wait_emptied(dve, ("out", n, t))
                    tt(x_tok[:, t, n * NC:(n + 1) * NC], x_tok[:, t, n * NC:(n + 1) * NC], t1, ALU.add).then_inc(h_res, 1)
                    if n == 0 and t < 2:
                        ada_sum(10 + t, la[:, t])
                if n == 0:
                    for i in (10, 11):
                        ada_row(i, mods[:, i - 4])
            dve.wait_ge(n2_in, 16)
            own(stt(row_a[:], mods[:, 4:6].rearrange("p a n -> p (a n)"), 1.0, row_a[:], ALU.add, ALU.mult))
            own.settle()
            for t in range(TT):
                dve.wait_ge(roots2, t + 1)
                own(dve.reciprocal(rstd[:, 4 + t:5 + t], rstd[:, 4 + t:5 + t]))
                own.settle()
                if t >= 2:
                    wait_job(dve, ("u2T", t - 2, 1))
                    dve.wait_ge(u2_out[t % 2], 16 * (t // 2))
                own(stt(tmp_tok[:, t % 2], x_tok[:, t], rstd[:, 4 + t:5 + t], row_a[:], ALU.mult, ALU.mult))
                own.settle()
                tt(tmp_tok[:, t % 2], tmp_tok[:, t % 2], mods[:, 2:4].rearrange("p a n -> p (a n)"), ALU.add).then_inc(u2_ready, 1)
            dve.wait_ge(router_in, 32)
            for t in range(TT):
                wait_emptied(dve, ("router", t))
                own(tt(sel[:, t], scores[:, t], bias_row[:], ALU.add))
                own.settle()
                own(dve.max(top8[:, t], sel[:, t]))
                own.settle()
                own(dve.match_replace(slot[:, t], top8[:, t], sel[:, t], -3e38))
                own.settle()
                own(tt(mask[:, t], slot[:, t], sel[:, t], ALU.not_equal))
                own.settle()
                dve.tensor_copy(mask_b[:, t], mask[:, t]).then_inc(mask_ready, 1)
                own(tt(w_left[:, t], scores[:, t], mask[:, t], ALU.mult))
                own.settle()
                own(dve.tensor_reduce(got[:, t:t + 1], w_left[:, t], AX_X, ALU.add))
                own.settle()
                own(dve.reciprocal(got[:, t:t + 1], got[:, t:t + 1]))
                own.settle()
                own(ts(w_left[:, t], w_left[:, t], got[:, t:t + 1], ROUTED_SCALE, ALU.mult, ALU.mult))
                own.settle()
            for i in range(3):
                own(dve.tensor_copy(w3[:, :, :, i], w_left[:]))
                own.settle()
                if i < 2:
                    own(tt(w_left[:], w_left[:], w3[:, :, :, i], ALU.subtract))
                    own.settle()
            for t in range(TT):
                wait_job(dve, ("sgu", t))
                dve.wait_ge(sgate_ready, t + 1)
                tt(sh_tok[:, t], sgate, bank(("sgu", t))[:, DE:2 * DE], ALU.mult).then_inc(dve_emptied, 1)
            wait_job(dve, "count")
            dve.tensor_copy(n_col[:, 0:1], bank("count")[:, 0:1]).then_inc(dve_emptied, 1)
            wait_emptied(dve, "count")
            own(ts(n_col[:, 4:8], block_start[:, 0:TT], n_col[:, 0:1], None, ALU.is_lt))
            own.settle()
            own(dve.tensor_reduce(n_col[:, 1:2], n_col[:, 4:8], AX_X, ALU.add))
            own.settle()
            ts(nb_rep[:], ones_b[:], n_col[:, 1:2], None, ALU.mult).then_inc(nb_ready, 1)
            wait_job(dve, "pos")
            dve.tensor_copy(slot[:].rearrange("p t e -> p (t e)"), bank("pos")).then_inc(dve_emptied, 1)
            wait_job(dve, "bstart_col")
            tt(n_col[:, 3:4], bank("bstart_col")[:, 0:1], n_col[:, 1:2], ALU.add).then_inc(dve_emptied, 1)
            wait_emptied(dve, "bstart_col")
            own(ts(n_col[:, 3:4], n_col[:, 3:4], float(P), None, ALU.mult))
            own.settle()
            wait_job(dve, "bstart_row")
            ts(sel[:, 0], bank("bstart_row")[:, 0:E], float(P), 1.0, ALU.mult, ALU.add).then_inc(dve_emptied, 1)
            wait_emptied(dve, "bstart_row")
            ts(over[:], block_start[:], n_col[:, 3:4], None, ALU.is_ge).then_inc(over_ready, 1)
            for t in range(TT):
                own(tt(slot[:, t], slot[:, t], sel[:, 0], ALU.add))
            own.settle()
            own(tt(slot[:], slot[:], mask[:], ALU.mult))
            own.settle()
            own(ts(slot[:], slot[:], -1.0, None, ALU.add))
            wait_job(dve, "table")
            own(ts(live_row, bank("table")[0:1, 0:TABLE], float(E), None, ALU.is_lt))
            own.settle()
            own(dve.tensor_reduce(n_col[0:1, 2:3], live_row, AX_X, ALU.add))
            own.settle()
            own(dve.tensor_copy(live_count[:], n_col[0:1, 2:3]))
            own(ts(live_of[0:1, :], bank("table")[0:1, 0:TABLE], float(E), None, ALU.is_lt))
            ts(expert_row[:, 0:TABLE], bank("table")[0:1, 0:TABLE], float(E - 1), None, ALU.min).then_inc(dve_emptied, 1)
            wait_emptied(dve, "table")
            own(dve.tensor_copy(expert_of, expert_row[:, 0:TABLE]))
            own(dve.memset(fresh_row[:, 0:1], 1.0))
            own(tt(fresh_row[:, 1:TABLE], expert_row[:, 1:TABLE], expert_row[:, 0:TABLE - 1], ALU.not_equal))
            own.settle()
            own(tt(fresh_row[:, 0:TABLE], fresh_row[:, 0:TABLE], live_row, ALU.mult))
            own.settle()
            own(dve.tensor_copy(fresh_of, fresh_row[:, 0:TABLE]))
            own.settle()
            own(dve.tensor_tensor_scan(live_row, fresh_row[:, 0:TABLE], fresh_row[:, 0:TABLE], -1.0, ALU.add, ALU.bypass))
            own.settle()
            own(dve.tensor_copy(order_of, live_row))
            dve.wait_ge(xg_zero, 2)
            own(dve.tensor_copy(pick_cols[:, :, 0:2], tok_cols[:]))
            own.settle()
            dve.nop().then_inc(tables_ready, 1)

            def pick_rows(n):
                e = dve.value_load(expert_of[0:1, bass.ds(n, 1)], min_val=0, max_val=E - 1)
                if not isinstance(n, int) or n:
                    dve.wait_ge(idx_psum, n)
                for t in range(TT):
                    own_loop = ts(pick[:, t], iota_row[:], block_start[:, bass.ds(n, 1)], slot[:, t, bass.ds(e, 1)], ALU.add, ALU.is_equal)
                    own_loop.then_inc(pick_ready, 1)
                dve.tensor_copy(pick_cols[:, :, 2:5], w3[:, :, bass.ds(e, 1), :].rearrange("p t o w -> p t (o w)")).then_inc(pick_ready, 1)

            def find_rows(n, s):
                dve.wait_ge(idx_psum, n + 1)
                dve.tensor_copy(got[:, 0:5], moe_bank(IDX)[:, 0:5]).then_inc(found, 1)
                dve.wait_ge(found, 4 * n + 1)
                stt(got[:, 5:6], got[:, 0:1], -1.0, got[:, 1:2], ALU.add, ALU.add).then_inc(found, 1)
                dve.wait_ge(found, 4 * n + 2)
                stt(got[:, 6:7], got[:, 5:6], 0.0, dummy_row[:], ALU.is_lt, ALU.mult).then_inc(found, 1)
                stt(row_w[:, s:s + 1], got[:, 2:3], got[:, 3:4], got[:, 4:5], ALU.add, ALU.add).then_inc(found, 1)
                dve.wait_ge(found, 4 * n + 4)
                tt(row_idx[:, s], got[:, 5:6], got[:, 6:7], ALU.add).then_inc(idx_ready, 1)

            def rows_lo(n):
                for g in range(2):
                    dve.wait_ge(xT_hi_ready, 2 * n + 1 + g)
                    tt(xT_lo[:, 4 * g:4 * g + 4], moe_bank(g).rearrange("p (k n) -> p k n", k=4), xT_hi[:, 4 * g:4 * g + 4].bitcast(F32), ALU.subtract).then_inc(xT_ready, 1)

            def expert_lo(n):
                fresh = dve.value_load(fresh_of[0:1, bass.ds(n, 1)], min_val=0, max_val=1)
                with dve.If(fresh > 0):
                    order = dve.value_load(order_of[0:1, bass.ds(n, 1)], min_val=0, max_val=E)
                    for p in range(PIECES):
                        dve.wait_ge(gu_hi_ready, order * PIECES + p + 1)
                        at = (slice(None), bass.ds(order % 2, 1), slice(PK * p, PK * p + PK))
                        tt(gu_lo[at].rearrange("p o k f -> p (o k) f"), gu_raw[:, PK * p:PK * p + PK],
                           gu_hi[at].rearrange("p o k f -> p (o k) f").bitcast(F32), ALU.subtract).then_inc(gu_split, 1)

            dve.nop().then_inc(h_ready, 1)
            dve.nop().then_inc(gu_split, PIECES)
            for n in range(2):
                pick_rows(n)
                find_rows(n, n)
            pick_rows(2)
            expert_lo(0)
            expert_lo(1)
            rows_lo(0)
            for i, s, b in live_blocks(dve):
                dve.wait_ge(silu_done, b + 1)
                dve.wait_ge(hT_psum, b + 1)
                tt(h_tok, gate_h, moe_bank(GU)[:, DE:2 * DE], ALU.mult).then_inc(h_ready, 1)
                dve.wait_ge(hT_psum, b + 2)
                dve.wait_ge(y_psum, 2 * b + 2)
                dve.tensor_copy(hT, moe_bank(HT)[:, 0:2 * P].rearrange("p (j n) -> p j n", j=2)).then_inc(hT_ready, 1)
                rows_lo(b + 1)
                dve.wait_ge(y_ready, 2 * b + 2)
                dve.tensor_copy(add_idx[:, s], row_idx[:, s]).then_inc(add_ready, 1)
                find_rows(b + 2, (s + 2) % UNROLL)
                expert_lo(b + 2)
                pick_rows(b + 3)
            dve.wait_ge(sum_in, 16)
            for t in range(TT):
                own2 = tt(sum_tok[:, t], sum_tok[:, t], g2_row, ALU.mult)
                own(own2)
                own.settle()
                tt(x_tok[:, t], x_tok[:, t], sum_tok[:, t], ALU.add).then_inc(h2_res, 1)
            dve.wait_ge(fg_in, 16)
            for t in range(TT):
                dve.wait_ge(roots3, t + 1)
                own(dve.reciprocal(rstd[:, t:t + 1], rstd[:, t:t + 1]))
                own.settle()
                stt(x_tok[:, t], x_tok[:, t], rstd[:, t:t + 1], row_a[:], ALU.mult, ALU.mult).then_inc(out_ready, 1)

        @block.tensor
        def _(pe):
            def start_job(name):
                n = J[name]
                if n >= BANKS:
                    wait_emptied(pe, jobs[n - BANKS][0])

            def end_job(ins):
                ins.then_inc(job_done, 1)

            def product(name, lhs, rhs, dst=None, tiles=KT):
                start_job(name)
                dst = bank(name) if dst is None else dst
                for k in range(tiles):
                    mm = pe.matmul(dst, lhs(k), rhs(k), start=(k == 0), stop=(k == tiles - 1))
                end_job(mm)

            def turn(name, src, tiles):
                start_job(name)
                for i, k in enumerate(tiles):
                    mm = pe.transpose(bank(name)[:, i * P:(i + 1) * P], src(k), ident[:])
                end_job(mm)

            def split_jobs(name, names, acts_hi, acts_lo, tokens_out):
                for j, job in enumerate(names):
                    start_job(job)
                    cols = slice(j * P, (j + 1) * P)
                    for k in range(KT):
                        p = k // PK
                        if j == 0 and k % PK == 0:
                            pe.wait_ge(pieces_done, PIECES * C[name] + p + 1)
                        at = place_of(name, p)
                        for n, (w, acts) in enumerate(((w_hi, acts_hi), (w_hi, acts_lo), (w_lo, acts_hi))):
                            lhs, rhs = w[:, at, k % PK], acts[:, k]
                            lhs, rhs = (rhs[:, cols], lhs) if tokens_out else (lhs[:, cols], rhs)
                            mm = pe.matmul(bank(job), lhs, rhs, start=(k == 0 and n == 0), stop=(k == KT - 1 and n == 2))
                        if j == 3 and k % PK == PK - 1 and p < PIECES - 1:
                            mm.then_inc(split_used, 1)
                    end_job(mm)

            def feature_major(name, acts_hi=uT_hi, acts_lo=uT_lo):
                split_jobs(name, [(name[0], j) for j in range(4 * name[1], 4 * name[1] + 4)], acts_hi, acts_lo, False)

            def token_major(name, names, acts_hi=uT_hi, acts_lo=uT_lo):
                split_jobs(name, names, acts_hi, acts_lo, True)

            def ada_product(i, acc):
                start_job(("ada", i))
                pe.wait_ge(pieces_done, PIECES * C[("ada", i)] + PIECES)
                end_job(pe.matmul(bank(("ada", i)), ones[:], acc, start=True, stop=True))

            pe.wait_ge(consts_ready, 1)
            pe.wait_ge(rows_in, 16 * 6)
            start_job("vectors")
            end_job(pe.transpose(bank("vectors")[:, 0:72], vec_rows, ident[0:72, 0:72]))
            for i in range(4):
                ada_product(i, tmpT[:, i % 2])
            for t in range(TT):
                pe.wait_ge(u_ready, t + 1)
                for g in range(2):
                    turn(("uT", t, g), lambda k: tmp_tok[:, t % 2, k * P:(k + 1) * P], range(4 * g, 4 * g + 4))
            wait_emptied(pe, ("uT", TT - 1, 1))
            pe.wait_ge(lr_split, 2)
            start_job("lr")
            for k in range(KT):
                for n, (w, acts) in enumerate(((wlr_hi, uT_hi), (wlr_hi, uT_lo), (wlr_lo, uT_hi))):
                    mm = pe.matmul(bank("lr")[0:RANK, :], w[:, k], acts[:, k], start=(k == 0 and n == 0), stop=(k == KT - 1 and n == 2))
            end_job(mm)
            wait_emptied(pe, "lr")
            for t in range(TT):
                product(("gate", t), lambda k: lrT[0:RANK + 1, t * P:(t + 1) * P], lambda k: wup[0:RANK + 1, :], tiles=1)
            for n in range(2):
                token_major(("v", n), [("v", n, t) for t in range(TT)])
            for t in range(TT):
                pe.wait_ge(la_ready, t + 1)
                product(("rem", t), lambda k: later[:], lambda k: la[:, t], tiles=1)
            start_job("tot")
            for h in range(HEADS):
                for t in range(TT):
                    at = h * NCHUNK + 2 * t
                    mm = pe.matmul(bank("tot")[:, at:at + 2], la[:, t, h * DK:(h + 1) * DK], in_chunk[:], start=True, stop=True)
            end_job(mm)
            token_major(("k", 0), [("k", t) for t in range(TT)])
            feature_major(("q", 0))
            for n in range(NCHUNK + 1):
                if n < NCHUNK:
                    t, lo = n // 2, (n % 2) * CHUNK
                    wait_emptied(pe, ("k", t))
                    for g in range(2):
                        start_job(("kv", n, g))
                        for h in range(2 * g, 2 * g + 2):
                            mm = pe.matmul(bank(("kv", n, g))[:, (h % 2) * DV:(h % 2 + 1) * DV], er[lo:lo + CHUNK, t, h * DK:(h + 1) * DK],
                                           v_tok[lo:lo + CHUNK, t, h * DV:(h + 1) * DV], start=True, stop=True)
                        end_job(mm)
                if n >= 1:
                    m = n - 1
                    wait_emptied(pe, ("kv", m, 1))
                    wait_emptied(pe, ("q", HEADS - 1))
                    start_job(("o", m))
                    for j in range(KT):
                        mm = pe.matmul(bank(("o", m))[:, j * CHUNK:(j + 1) * CHUNK], state[:, m % 2, j // 2, (j % 2) * P:(j % 2 + 1) * P],
                                       qT[:, j // 2, m * CHUNK:(m + 1) * CHUNK], start=True, stop=True)
                    end_job(mm)
            for n in range(2):
                feature_major(("rx", n))
                if n == 0:
                    for h in range(HEADS):
                        pe.wait_ge(sq_ready, h + 1)
                        product(("ss", h), lambda k: ones[:], lambda k: tmpT[:, 2 * (h % 2) + k], tiles=2)
                    pe.wait_ge(gates_in, 32)
                for j in range(4 * n, 4 * n + 4):
                    wait_emptied(pe, ("rx", j))
                    for i, name in enumerate(("ra", "ri")):
                        product((name, j), lambda k: gate_w[:, i, j], lambda k: xr[:, j % 4], tiles=1)
            for name in ("rg", "og"):
                for n in range(2):
                    feature_major((name, n))
            for gate, y in (("gb", "yb"), ("ga", "ya")):
                for n in range(2):
                    feature_major((gate, n))
                    for i in ADA_AFTER.get((gate, n), ()):
                        ada_product(i, la[:, i % 2])
                    pe.wait_ge(o_split if y == "yb" else hg_split, KT)
                    feature_major((y, n), o_hi, o_lo)
                    for i in ADA_AFTER.get((y, n), ()):
                        ada_product(i, la[:, i % 2])
            pe.wait_ge(m_split, KT)
            for n in range(2):
                token_major(("out", n), [("out", n, t) for t in range(TT)])
                for i in ADA_AFTER.get(("out", n), ()):
                    ada_product(i, la[:, i % 2])
            for t in range(TT):
                pe.wait_ge(u2_ready, t + 1)
                for g in range(2):
                    turn(("u2T", t, g), lambda k: tmp_tok[:, t % 2, k * P:(k + 1) * P], range(4 * g, 4 * g + 4))
            pe.wait_ge(router_in, 32)
            for t in range(TT):
                wait_emptied(pe, ("u2T", t, 1))
                product(("router", t), lambda k: u2T[:, k, t * P:(t + 1) * P], lambda k: router[:, k], dst=bank(("router", t))[:, 0:E])
            pe.wait_ge(shared_in[0], 16)
            for t in range(TT):
                product(("sgu", t), lambda k: u2T[:, k, t * P:(t + 1) * P], lambda k: sgu_w[:, k])
            pe.wait_ge(mask_ready, TT)
            product("count", lambda t: mask_b[:, t], lambda t: ones_b[:, 0:1], dst=bank("count")[:, 0:1], tiles=TT)
            start_job("pos")
            for t in range(TT):
                for i in range(t + 1):
                    mm = pe.matmul(bank("pos")[:, t * E:(t + 1) * E], tri[:] if i == t else ones_b[:], mask_b[:, i], start=(i == 0), stop=(i == t))
            end_job(mm)
            pe.wait_ge(nb_ready, 1)
            product("bstart_col", lambda k: tri[:], lambda k: nb_rep[:, 0:1], dst=bank("bstart_col")[:, 0:1], tiles=1)
            product("bstart_row", lambda k: nb_rep[:], lambda k: tri[:], dst=bank("bstart_row")[:, 0:E], tiles=1)
            pe.wait_ge(over_ready, 1)
            product("table", lambda k: ones_b[:, 0:1], lambda k: over[:], dst=bank("table")[0:1, 0:TABLE], tiles=1)
            for t in range(TT):
                wait_emptied(pe, ("sgu", t))
                turn(("shT", t), lambda k: sh_tok[:, t, k * P:(k + 1) * P], range(2))
            pe.wait_ge(shared_in[1], 16)
            wait_emptied(pe, ("shT", TT - 1))
            for n in range(2):
                for t in range(TT):
                    product(("sdown", n, t), lambda k: shT[:, k, t * P:(t + 1) * P], lambda k: sdown_w[:, k, n * NC:(n + 1) * NC], tiles=2)

            def find(n):
                pe.wait_ge(pick_ready, 5 * n + 5)
                if not isinstance(n, int) or n:
                    pe.wait_ge(idx_ready, n)
                for t in range(TT):
                    mm = pe.matmul(moe_bank(IDX)[:, 0:5], pick[:, t], pick_cols[:, t], start=(t == 0), stop=(t == TT - 1))
                mm.then_inc(idx_psum, 1)

            def turn_rows(n, s, uses, tiles=range(KT)):
                pe.wait_ge(gathered[s], uses)
                for k in tiles:
                    mm = pe.transpose(moe_bank(k // 4)[:, (k % 4) * P:(k % 4 + 1) * P], xg[:, s, bass.ds(k, P, KT)], ident[:])
                    if k % 4 == 3:
                        mm.then_inc(xT_psum, 1)

            pe.wait_ge(act_emptied, emptied_by.count("act"))
            pe.wait_ge(dve_emptied, emptied_by.count("dve"))
            pe.wait_ge(tables_ready, 1)
            pe.nop().then_inc(hT_psum, 1)
            pe.nop().then_inc(y_psum, 2)
            find(0)
            find(1)
            turn_rows(0, 0, 16)
            for i, s, b in live_blocks(pe):
                order = pe.value_load(order_of[0:1, bass.ds(b, 1)], min_val=0, max_val=E)
                place, gu_place = bass.ds(order % UNROLL, 1), bass.ds(order % 2, 1)
                pe.wait_ge(xT_ready, 2 * b + 2)
                pe.wait_ge(gu_split, order * PIECES + 2 * PIECES)
                for k in range(KT):
                    for n, (w, rows) in enumerate(((gu_hi, xT_hi), (gu_lo, xT_hi), (gu_hi, xT_lo))):
                        mm = pe.matmul(moe_bank(GU), rows[:, k], w[:, gu_place, k].rearrange("p o n -> p (o n)"),
                                       start=(k == 0 and n == 0), stop=(k == KT - 1 and n == 2))
                mm.then_inc(gu_done, 1)
                after = (s + 1) % UNROLL, 16 * i + 16 + 16 * ((s + 1) // UNROLL)
                turn_rows(b + 1, *after, tiles=range(6))
                pe.wait_ge(h_ready, b + 2)
                for j in range(2):
                    mm = pe.transpose(moe_bank(HT)[:, j * P:(j + 1) * P], h_tok[:, j * P:(j + 1) * P], ident[:])
                mm.then_inc(hT_psum, 1)
                turn_rows(b + 1, *after, tiles=range(6, KT))
                find(b + 2)
                pe.wait_ge(hT_ready, b + 1)
                pe.wait_ge(w_loaded[s], 16 * i + 16)
                pe.wait_ge(y_ready, 2 * b + 2)
                for g in range(2):
                    for j in range(2):
                        mm = pe.matmul(moe_bank(Y0 + g), hT[:, j], w_dn[:, place, j, g * NC:(g + 1) * NC].rearrange("p o n -> p (o n)"), start=(j == 0), stop=(j == 1))
                    mm.then_inc(y_psum, 1)



_INS = ["x", "c", "ada_w", "ada_b", "norm1_g", "w_in", "conv_w", "conv_b", "rg_wa", "rg_ba", "rg_wx", "rg_bx",
        "rg_lambda", "gla_w_up", "gla_b_up", "gla_norm_g", "w_branch_a", "w_branch_b", "w_out", "norm2_g",
        "router_w", "router_b", "exp_w_gu", "exp_w_down", "shared_w_gu", "shared_w_down", "final_g"]


def kernel(**inputs):
    import numpy as _np
    import concourse.bacc as _bacc
    from concourse import mybir as _mybir
    from concourse.bass_utils import run_bass_kernel_spmd as _run

    nc = _bacc.Bacc("TRN2", target_bir_lowering=False, num_devices=1)
    arrays, args = {}, []
    for name in _INS:
        a = _np.ascontiguousarray(inputs[name])
        arrays[f"in_{name}"] = a
        args.append(nc.dram_tensor(f"in_{name}", a.shape, _mybir.dt.from_np(a.dtype), kind="ExternalInput").ap())
    result = nc.dram_tensor("result", (1, T, D), _mybir.dt.float32, kind="ExternalOutput").ap()
    layer_program(nc, *args, result)
    r = _run(nc, [arrays], core_ids=[0])
    return r.results[0]["result"]
```
